# Optimizing a Trainium2 kernel written in Bass

```python
import jax, jax.numpy as jnp
from jax import lax
import numpy as np
import math

D_MODEL = 1024
BATCH = 1
SEQ = 256
DEPTH = 2

N_SUB = 3
HALF_STEP = 0.5
D_FF = 2816
CONV_WIDTH = 4
EPS = 1e-6
LRU_WIDTH = D_MODEL
LRU_HEADS = 8
LRU_BLOCK = LRU_WIDTH // LRU_HEADS
LRU_C = 8.0
SSD_WIDTH = D_MODEL
SSD_HEADDIM = 64
SSD_HEADS = SSD_WIDTH // SSD_HEADDIM
SSD_GROUPS = 2
SSD_STATE = 128
SSD_CHUNK = 128
SSD_CONV_DIM = SSD_WIDTH + 2 * SSD_GROUPS * SSD_STATE
HYB_SPLITS = (LRU_WIDTH, 2 * LRU_WIDTH, 2 * LRU_WIDTH + SSD_WIDTH, 2 * LRU_WIDTH + SSD_WIDTH + SSD_CONV_DIM)
HYB_IN = HYB_SPLITS[-1] + SSD_HEADS
HYB_OUT = LRU_WIDTH + SSD_WIDTH
MLSTM_WIDTH = 2 * D_MODEL
MLSTM_HEADS = 4
MLSTM_HEADDIM = MLSTM_WIDTH // MLSTM_HEADS
MLSTM_QKV_BLOCK = 4
MLSTM_CHUNK = 64
N_EVEN = (DEPTH + 1) // 2
N_ODD = DEPTH // 2


def rms_norm(x, g):
    xf = x.astype(jnp.float32)
    y = xf * lax.rsqrt(jnp.mean(xf * xf, axis=-1, keepdims=True) + EPS)
    return (y * g.astype(jnp.float32)).astype(x.dtype)

def head_layer_norm(h, g):
    mu = jnp.mean(h, axis=-1, keepdims=True)
    hc = h - mu
    var = jnp.mean(hc * hc, axis=-1, keepdims=True)
    return hc * lax.rsqrt(var + EPS) * g.astype(jnp.float32)

def causal_conv(x, w, b):
    width, ch = w.shape
    y = lax.conv_general_dilated(x, w[:, None, :].astype(x.dtype), window_strides=(1,),
                                 padding=((width - 1, 0),), dimension_numbers=('NWC', 'WIO', 'NWC'),
                                 feature_group_count=ch)
    return y + b

def block_diag_linear(x, w):
    nb, bi, bo = w.shape
    xb = x.reshape(x.shape[:-1] + (nb, bi))
    return jnp.einsum('...ni,nio->...no', xb, w).reshape(x.shape[:-1] + (nb * bo,))

def swiglu(h, w_gate, w_up, w_down):
    return (jax.nn.silu(h @ w_gate) * (h @ w_up)) @ w_down

def rg_lru(x, w_a, b_a, w_x, b_x, lam):
    xf = x.astype(jnp.float32)
    r = jax.nn.sigmoid(block_diag_linear(xf, w_a.astype(jnp.float32)) + b_a.astype(jnp.float32))
    i = jax.nn.sigmoid(block_diag_linear(xf, w_x.astype(jnp.float32)) + b_x.astype(jnp.float32))
    log_a = -LRU_C * r * jax.nn.softplus(-lam.astype(jnp.float32))
    a = jnp.exp(log_a)
    u = jnp.sqrt(-jnp.expm1(2.0 * log_a)) * (i * xf)

    def combine(left, right):
        a_l, u_l = left
        a_r, u_r = right
        return a_l * a_r, a_r * u_l + u_r

    _, h = lax.associative_scan(combine, (a, u), axis=1)
    return h

def segsum(x):
    t = x.shape[-1]
    cs = jnp.cumsum(x, axis=-1)
    diff = cs[..., :, None] - cs[..., None, :]
    mask = jnp.tril(jnp.ones((t, t), dtype=bool))
    return jnp.where(mask, diff, -jnp.inf)

def ssd_chunked(x, dt, a, bm, cm):
    bsz, seq, nh, hp = x.shape
    ng, ns = bm.shape[-2:]
    ne = nh // ng
    nc = seq // SSD_CHUNK
    ln = SSD_CHUNK
    xc = (x * dt[..., None]).reshape(bsz, nc, ln, ng, ne, hp)
    bc = bm.reshape(bsz, nc, ln, ng, ns)
    cc = cm.reshape(bsz, nc, ln, ng, ns)
    ac = (dt * a).reshape(bsz, nc, ln, ng, ne).transpose(0, 3, 4, 1, 2)
    acs = jnp.cumsum(ac, axis=-1)
    decay_in = jnp.exp(segsum(ac))
    cb = jnp.einsum('bclgn,bcsgn->bgcls', cc, bc)
    y_diag = jnp.einsum('bgecls,bcsgep->bclgep', cb[:, :, None] * decay_in, xc)
    decay_states = jnp.exp(acs[..., -1:] - acs).transpose(0, 3, 4, 1, 2)
    states = jnp.einsum('bclgn,bclgep->bcgepn', bc, xc * decay_states[..., None])
    chunk_tot = jnp.pad(acs[..., -1], ((0, 0), (0, 0), (0, 0), (1, 0)))
    decay_chunk = jnp.exp(segsum(chunk_tot))
    states = jnp.pad(states, ((0, 0), (1, 0), (0, 0), (0, 0), (0, 0), (0, 0)))
    prev_states = jnp.einsum('bgezj,bjgepn->bzgepn', decay_chunk, states)[:, :-1]
    decay_out = jnp.exp(acs).transpose(0, 3, 4, 1, 2)
    y_off = jnp.einsum('bclgn,bcgepn->bclgep', cc, prev_states) * decay_out[..., None]
    return (y_diag + y_off).reshape(bsz, seq, nh, hp)

def mlstm_chunkwise(q, k, v, i_pre, f_pre):
    bsz, nh, seq, dh = q.shape
    nc = seq // MLSTM_CHUNK
    ln = MLSTM_CHUNK
    k = k * (dh ** -0.5)
    log_f = jax.nn.log_sigmoid(f_pre)

    def to_chunks(t):
        return jnp.moveaxis(t.reshape((bsz, nh, nc, ln) + t.shape[3:]), 2, 0)

    causal = jnp.tril(jnp.ones((ln, ln), dtype=bool))

    def step(carry, inp):
        c_st, n_st, m_st = carry
        q_c, k_c, v_c, i_c, lf_c = inp
        bcum = jnp.cumsum(lf_c, axis=-1)
        log_d = jnp.where(causal, bcum[..., :, None] - bcum[..., None, :] + i_c[..., None, :], -jnp.inf)
        g = bcum + m_st[..., None]
        m = jnp.maximum(g, jnp.max(log_d, axis=-1))
        w_inter = jnp.exp(g - m)
        s_mat = jnp.einsum('bhtd,bhsd->bhts', q_c, k_c) * jnp.exp(log_d - m[..., None])
        num = w_inter[..., None] * jnp.einsum('bhtd,bhdv->bhtv', q_c, c_st) + jnp.einsum('bhts,bhsv->bhtv', s_mat, v_c)
        den = w_inter * jnp.einsum('bhtd,bhd->bht', q_c, n_st) + jnp.sum(s_mat, axis=-1)
        h_out = num / jnp.maximum(jnp.abs(den), jnp.exp(-m))[..., None]
        b_last = bcum[..., -1]
        log_w = b_last[..., None] - bcum + i_c
        m_new = jnp.maximum(b_last + m_st, jnp.max(log_w, axis=-1))
        w_s = jnp.exp(log_w - m_new[..., None])
        decay = jnp.exp(b_last + m_st - m_new)
        c_new = decay[..., None, None] * c_st + jnp.einsum('bhs,bhsd,bhsv->bhdv', w_s, k_c, v_c)
        n_new = decay[..., None] * n_st + jnp.einsum('bhs,bhsd->bhd', w_s, k_c)
        return (c_new, n_new, m_new), h_out

    init = (jnp.zeros((bsz, nh, dh, dh), jnp.float32), jnp.zeros((bsz, nh, dh), jnp.float32),
            jnp.zeros((bsz, nh), jnp.float32))
    _, hc = lax.scan(step, init, (to_chunks(q), to_chunks(k), to_chunks(v), to_chunks(i_pre), to_chunks(log_f)))
    return jnp.moveaxis(hc, 0, 2).reshape(bsz, nh, seq, dh)

def hybrid_mixer(h, w_in, w_out, lru_conv_w, lru_conv_b, lru_wa, lru_ba, lru_wx, lru_bx, lru_lambda,
                 ssd_conv_w, ssd_conv_b, ssd_dt_bias, ssd_a_log, ssd_d, ssd_norm_g):
    bsz, seq, _ = h.shape
    f32 = jnp.float32
    gate_lru, x_lru, z_ssd, xbc, dt_raw = jnp.split(h @ w_in, HYB_SPLITS, axis=-1)
    x_lru = causal_conv(x_lru, lru_conv_w, lru_conv_b)
    y_lru = rg_lru(x_lru, lru_wa, lru_ba, lru_wx, lru_bx, lru_lambda) * jax.nn.gelu(gate_lru.astype(f32))
    xbc = jax.nn.silu(causal_conv(xbc, ssd_conv_w, ssd_conv_b)).astype(f32)
    gn = SSD_GROUPS * SSD_STATE
    xs = xbc[..., :SSD_WIDTH].reshape(bsz, seq, SSD_HEADS, SSD_HEADDIM)
    bm = xbc[..., SSD_WIDTH:SSD_WIDTH + gn].reshape(bsz, seq, SSD_GROUPS, SSD_STATE)
    cm = xbc[..., SSD_WIDTH + gn:].reshape(bsz, seq, SSD_GROUPS, SSD_STATE)
    dt = jax.nn.softplus(dt_raw.astype(f32) + ssd_dt_bias.astype(f32))
    a = -jnp.exp(ssd_a_log.astype(f32))
    y = ssd_chunked(xs, dt, a, bm, cm) + ssd_d.astype(f32)[:, None] * xs
    y = y.reshape(bsz, seq, SSD_WIDTH) * jax.nn.silu(z_ssd.astype(f32))
    y = rms_norm(y.reshape(bsz, seq, SSD_GROUPS, SSD_WIDTH // SSD_GROUPS),
                 ssd_norm_g.reshape(SSD_GROUPS, SSD_WIDTH // SSD_GROUPS)).reshape(bsz, seq, SSD_WIDTH)
    y_cat = jnp.concatenate([y_lru, y], axis=-1).astype(h.dtype)
    return y_cat @ w_out

def mlstm_block(h, w_up, conv_w, conv_b, wq, wk, wv, w_gates, b_gates, norm_g, skip, w_down):
    bsz, seq, _ = h.shape
    f32 = jnp.float32
    xm, z = jnp.split(h @ w_up, 2, axis=-1)
    xc = jax.nn.silu(causal_conv(xm, conv_w, conv_b))
    q = block_diag_linear(xc, wq)
    k = block_diag_linear(xc, wk)
    v = block_diag_linear(xm, wv)
    gates = (q @ w_gates[:MLSTM_WIDTH] + k @ w_gates[MLSTM_WIDTH:2 * MLSTM_WIDTH]
             + v @ w_gates[2 * MLSTM_WIDTH:] + b_gates).astype(f32).transpose(0, 2, 1)
    i_pre = gates[:, :MLSTM_HEADS]
    f_pre = gates[:, MLSTM_HEADS:]

    def heads(t):
        return t.astype(f32).reshape(bsz, seq, MLSTM_HEADS, MLSTM_HEADDIM).transpose(0, 2, 1, 3)

    hh = mlstm_chunkwise(heads(q), heads(k), heads(v), i_pre, f_pre)
    hh = head_layer_norm(hh.transpose(0, 2, 1, 3), norm_g.reshape(MLSTM_HEADS, MLSTM_HEADDIM))
    hh = hh.reshape(bsz, seq, MLSTM_WIDTH) + skip.astype(f32) * xc.astype(f32)
    return (hh * jax.nn.silu(z.astype(f32))).astype(h.dtype) @ w_down

def first_inputs(seed: int = 0) -> dict:
    key = jax.random.key(seed)
    ks = iter(jax.random.split(key, 64))
    f32 = jnp.float32

    def nrm(shape, fan_in, scale=1.0):
        return jax.random.normal(next(ks), shape, f32) * (scale * fan_in ** -0.5)

    def small(shape, s=0.02):
        return jax.random.normal(next(ks), shape, f32) * s

    def gain(shape):
        return 1.0 + small(shape, 0.05)

    x = jax.random.normal(next(ks), (BATCH, SEQ, D_MODEL), f32)
    c = jax.random.normal(next(ks), (BATCH, D_MODEL), f32)
    ada_w = nrm((DEPTH, D_MODEL, N_SUB * 3 * D_MODEL), D_MODEL, 0.5)
    ada_b = small((DEPTH, N_SUB * 3 * D_MODEL))
    norm_g = gain((DEPTH, N_SUB, D_MODEL))
    ffn_w_gate = nrm((DEPTH, 2, D_MODEL, D_FF), D_MODEL)
    ffn_w_up = nrm((DEPTH, 2, D_MODEL, D_FF), D_MODEL)
    ffn_w_down = nrm((DEPTH, 2, D_FF, D_MODEL), D_FF)
    hyb_w_in = nrm((N_EVEN, D_MODEL, HYB_IN), D_MODEL)
    hyb_w_out = nrm((N_EVEN, HYB_OUT, D_MODEL), HYB_OUT)
    lru_conv_w = nrm((N_EVEN, CONV_WIDTH, LRU_WIDTH), CONV_WIDTH)
    lru_conv_b = small((N_EVEN, LRU_WIDTH))
    lru_wa = nrm((N_EVEN, LRU_HEADS, LRU_BLOCK, LRU_BLOCK), LRU_BLOCK)
    lru_ba = small((N_EVEN, LRU_WIDTH))
    lru_wx = nrm((N_EVEN, LRU_HEADS, LRU_BLOCK, LRU_BLOCK), LRU_BLOCK)
    lru_bx = small((N_EVEN, LRU_WIDTH))
    a_pow = jax.random.uniform(next(ks), (N_EVEN, LRU_WIDTH), f32, minval=0.9, maxval=0.999)
    s_a = a_pow ** (1.0 / LRU_C)
    lru_lambda = jnp.log(s_a) - jnp.log1p(-s_a)
    ssd_conv_w = nrm((N_EVEN, CONV_WIDTH, SSD_CONV_DIM), CONV_WIDTH)
    ssd_conv_b = small((N_EVEN, SSD_CONV_DIM))
    dt0 = jnp.exp(jax.random.uniform(next(ks), (N_EVEN, SSD_HEADS), f32,
                                     minval=float(np.log(1e-3)), maxval=float(np.log(1e-1))))
    ssd_dt_bias = dt0 + jnp.log(-jnp.expm1(-dt0))
    ssd_a_log = jnp.log(jax.random.uniform(next(ks), (N_EVEN, SSD_HEADS), f32, minval=1.0, maxval=16.0))
    ssd_d = gain((N_EVEN, SSD_HEADS))
    ssd_norm_g = gain((N_EVEN, SSD_WIDTH))
    mlstm_w_up = nrm((N_ODD, D_MODEL, 2 * MLSTM_WIDTH), D_MODEL)
    mlstm_conv_w = nrm((N_ODD, CONV_WIDTH, MLSTM_WIDTH), CONV_WIDTH)
    mlstm_conv_b = small((N_ODD, MLSTM_WIDTH))
    nblk = MLSTM_WIDTH // MLSTM_QKV_BLOCK
    mlstm_wq = nrm((N_ODD, nblk, MLSTM_QKV_BLOCK, MLSTM_QKV_BLOCK), MLSTM_QKV_BLOCK)
    mlstm_wk = nrm((N_ODD, nblk, MLSTM_QKV_BLOCK, MLSTM_QKV_BLOCK), MLSTM_QKV_BLOCK)
    mlstm_wv = nrm((N_ODD, nblk, MLSTM_QKV_BLOCK, MLSTM_QKV_BLOCK), MLSTM_QKV_BLOCK)
    mlstm_w_gates = nrm((N_ODD, 3 * MLSTM_WIDTH, 2 * MLSTM_HEADS), 3 * MLSTM_WIDTH, 0.5)
    f_bias = jnp.broadcast_to(jnp.linspace(3.0, 6.0, MLSTM_HEADS, dtype=f32), (N_ODD, MLSTM_HEADS))
    mlstm_b_gates = jnp.concatenate([small((N_ODD, MLSTM_HEADS), 0.1),
                                     f_bias + small((N_ODD, MLSTM_HEADS), 0.02)], axis=-1)
    mlstm_norm_g = gain((N_ODD, MLSTM_WIDTH))
    mlstm_skip = gain((N_ODD, MLSTM_WIDTH))
    mlstm_w_down = nrm((N_ODD, MLSTM_WIDTH, D_MODEL), MLSTM_WIDTH)
    final_norm_g = gain((D_MODEL,))
    return {'x': x, 'c': c, 'ada_w': ada_w, 'ada_b': ada_b, 'norm_g': norm_g,
            'ffn_w_gate': ffn_w_gate, 'ffn_w_up': ffn_w_up, 'ffn_w_down': ffn_w_down,
            'hyb_w_in': hyb_w_in, 'hyb_w_out': hyb_w_out,
            'lru_conv_w': lru_conv_w, 'lru_conv_b': lru_conv_b, 'lru_wa': lru_wa, 'lru_ba': lru_ba,
            'lru_wx': lru_wx, 'lru_bx': lru_bx, 'lru_lambda': lru_lambda,
            'ssd_conv_w': ssd_conv_w, 'ssd_conv_b': ssd_conv_b, 'ssd_dt_bias': ssd_dt_bias,
            'ssd_a_log': ssd_a_log, 'ssd_d': ssd_d, 'ssd_norm_g': ssd_norm_g,
            'mlstm_w_up': mlstm_w_up, 'mlstm_conv_w': mlstm_conv_w, 'mlstm_conv_b': mlstm_conv_b,
            'mlstm_wq': mlstm_wq, 'mlstm_wk': mlstm_wk, 'mlstm_wv': mlstm_wv,
            'mlstm_w_gates': mlstm_w_gates, 'mlstm_b_gates': mlstm_b_gates,
            'mlstm_norm_g': mlstm_norm_g, 'mlstm_skip': mlstm_skip, 'mlstm_w_down': mlstm_w_down,
            'final_norm_g': final_norm_g}

def first_block(x, c, ada_w, ada_b, norm_g, ffn_w_gate, ffn_w_up, ffn_w_down, hyb_w_in, hyb_w_out,
              lru_conv_w, lru_conv_b, lru_wa, lru_ba, lru_wx, lru_bx, lru_lambda,
              ssd_conv_w, ssd_conv_b, ssd_dt_bias, ssd_a_log, ssd_d, ssd_norm_g,
              mlstm_w_up, mlstm_conv_w, mlstm_conv_b, mlstm_wq, mlstm_wk, mlstm_wv,
              mlstm_w_gates, mlstm_b_gates, mlstm_norm_g, mlstm_skip, mlstm_w_down, final_norm_g):
    bsz = x.shape[0]
    c_act = jax.nn.silu(c)
    for layer in range(DEPTH):
        mod = (c_act @ ada_w[layer] + ada_b[layer]).reshape(bsz, N_SUB, 3, D_MODEL)[:, :, :, None, :]

        def modulate(t, sub):
            return rms_norm(t, norm_g[layer, sub]) * (1.0 + mod[:, sub, 1]) + mod[:, sub, 0]

        h = modulate(x, 0)
        x = x + HALF_STEP * (1.0 + mod[:, 0, 2]) * swiglu(h, ffn_w_gate[layer, 0], ffn_w_up[layer, 0], ffn_w_down[layer, 0])
        h = modulate(x, 1)
        if layer % 2 == 0:
            e = layer // 2
            y = hybrid_mixer(h, hyb_w_in[e], hyb_w_out[e], lru_conv_w[e], lru_conv_b[e], lru_wa[e], lru_ba[e],
                             lru_wx[e], lru_bx[e], lru_lambda[e], ssd_conv_w[e], ssd_conv_b[e],
                             ssd_dt_bias[e], ssd_a_log[e], ssd_d[e], ssd_norm_g[e])
        else:
            o = layer // 2
            y = mlstm_block(h, mlstm_w_up[o], mlstm_conv_w[o], mlstm_conv_b[o], mlstm_wq[o], mlstm_wk[o],
                            mlstm_wv[o], mlstm_w_gates[o], mlstm_b_gates[o], mlstm_norm_g[o],
                            mlstm_skip[o], mlstm_w_down[o])
        x = x + (1.0 + mod[:, 1, 2]) * y.astype(x.dtype)
        h = modulate(x, 2)
        x = x + HALF_STEP * (1.0 + mod[:, 2, 2]) * swiglu(h, ffn_w_gate[layer, 1], ffn_w_up[layer, 1], ffn_w_down[layer, 1])
    return rms_norm(x, final_norm_g)


DEPTH_2 = 4

N_MIXERS = 3
BLOCK = 128
ROPE_THETA = 10000.0
NORM_EPS = 1e-6

A_HEADS = 8
A_HEAD_DIM = D_MODEL // (2 * A_HEADS)
A_V_DIM = 2 * A_HEAD_DIM
A_IN = 4 * A_HEADS * A_HEAD_DIM + A_HEADS * A_V_DIM

B_HEADS = 16
B_HEAD_DIM = D_MODEL // B_HEADS
B_IN = 3 * B_HEADS * B_HEAD_DIM

C_HEADS = 16
C_KV_HEADS = 2
C_GROUP = C_HEADS // C_KV_HEADS
C_HEAD_DIM = 64
WINDOW = 128
C_IN = (C_HEADS + 2 * C_KV_HEADS) * C_HEAD_DIM

ROPE_DIM = 64

FFN_HIDDEN = -(-8 * D_MODEL // (3 * 256)) * 256

N_A = (DEPTH_2 + 2) // 3
N_B = (DEPTH_2 + 1) // 3
N_C = DEPTH_2 // 3


def rms_norm_2(x, g):
    xf = x.astype(jnp.float32)
    y = xf * lax.rsqrt(jnp.mean(xf * xf, axis=-1, keepdims=True) + NORM_EPS)
    return (y * g.astype(jnp.float32)).astype(x.dtype)

def rope_tables(positions):
    inv = ROPE_THETA ** (-jnp.arange(0, ROPE_DIM, 2, dtype=jnp.float32) / ROPE_DIM)
    ang = positions.astype(jnp.float32)[..., None] * inv
    return jnp.cos(ang), jnp.sin(ang)

def apply_rope(x, cos, sin):
    xf = x.astype(jnp.float32)
    x1, x2 = jnp.split(xf, 2, axis=-1)
    c = cos[:, :, None, :]
    s = sin[:, :, None, :]
    return jnp.concatenate([x1 * c - x2 * s, x2 * c + x1 * s], axis=-1).astype(x.dtype)

def diff_attention(h, w_in, w_out, lam_params, subln_g, cos, sin, layer_idx):
    b, s, _ = h.shape
    nblk = s // BLOCK
    qkv = h @ w_in
    nq = 2 * A_HEADS * A_HEAD_DIM
    q, k, v = jnp.split(qkv, [nq, 2 * nq], axis=-1)
    q = apply_rope(q.reshape(b, s, 2 * A_HEADS, A_HEAD_DIM), cos, sin).reshape(b, s, A_HEADS, 2, A_HEAD_DIM)
    k = apply_rope(k.reshape(b, s, 2 * A_HEADS, A_HEAD_DIM), cos, sin).reshape(b, s, A_HEADS, 2, A_HEAD_DIM)
    v = v.reshape(b, s, A_HEADS, A_V_DIM)
    lam_init = 0.8 - 0.6 * math.exp(-0.3 * layer_idx)
    lp = lam_params.astype(jnp.float32)
    lam = jnp.exp(jnp.sum(lp[0] * lp[1])) - jnp.exp(jnp.sum(lp[2] * lp[3])) + lam_init
    scale = A_HEAD_DIM ** -0.5
    kpos = jnp.arange(s)
    q_blocks = jnp.moveaxis(q.reshape(b, nblk, BLOCK, A_HEADS, 2, A_HEAD_DIM), 1, 0)

    def block(args):
        qb, i = args
        sc = jnp.einsum('bqhcd,bkhcd->bhcqk', qb, k).astype(jnp.float32) * scale
        qpos = i * BLOCK + jnp.arange(BLOCK)
        causal = kpos[None, :] <= qpos[:, None]
        p = jax.nn.softmax(jnp.where(causal, sc, -jnp.inf), axis=-1)
        wts = p[:, :, 0] - lam * p[:, :, 1]
        return jnp.einsum('bhqk,bkhe->bqhe', wts.astype(v.dtype), v)

    o = lax.map(block, (q_blocks, jnp.arange(nblk)))
    o = jnp.moveaxis(o, 0, 1).reshape(b, s, A_HEADS, A_V_DIM)
    o = rms_norm_2(o, subln_g) * (1.0 - lam_init)
    return o.reshape(b, s, A_HEADS * A_V_DIM) @ w_out

def stick_breaking_attention(h, w_in, w_out):
    b, s, _ = h.shape
    nblk = s // BLOCK
    qkv = h @ w_in
    q, k, v = jnp.split(qkv, 3, axis=-1)
    q = q.reshape(b, s, B_HEADS, B_HEAD_DIM)
    k = k.reshape(b, s, B_HEADS, B_HEAD_DIM)
    v = v.reshape(b, s, B_HEADS, B_HEAD_DIM)
    scale = B_HEAD_DIM ** -0.5
    kpos = jnp.arange(s)
    q_blocks = jnp.moveaxis(q.reshape(b, nblk, BLOCK, B_HEADS, B_HEAD_DIM), 1, 0)

    def block(args):
        qb, i = args
        z = jnp.einsum('bqhd,bkhd->bhqk', qb, k).astype(jnp.float32) * scale
        qpos = i * BLOCK + jnp.arange(BLOCK)
        strict = kpos[None, :] < qpos[:, None]
        log_beta = jax.nn.log_sigmoid(z)
        log_1m_beta = jnp.where(strict, jax.nn.log_sigmoid(-z), 0.0)
        suffix = lax.cumsum(log_1m_beta, axis=3, reverse=True) - log_1m_beta
        a = jnp.where(strict, jnp.exp(log_beta + suffix), 0.0)
        return jnp.einsum('bhqk,bkhd->bqhd', a.astype(v.dtype), v)

    o = lax.map(block, (q_blocks, jnp.arange(nblk)))
    o = jnp.moveaxis(o, 0, 1).reshape(b, s, B_HEADS * B_HEAD_DIM)
    return o @ w_out

def sliding_window_sink_attention(h, w_in, w_out, sinks, cos, sin):
    b, s, _ = h.shape
    nblk = s // WINDOW
    qkv = h @ w_in
    nq = C_HEADS * C_HEAD_DIM
    nkv = C_KV_HEADS * C_HEAD_DIM
    q, k, v = jnp.split(qkv, [nq, nq + nkv], axis=-1)
    q = apply_rope(q.reshape(b, s, C_HEADS, C_HEAD_DIM), cos, sin)
    k = apply_rope(k.reshape(b, s, C_KV_HEADS, C_HEAD_DIM), cos, sin)
    v = v.reshape(b, s, C_KV_HEADS, C_HEAD_DIM)
    qb = q.reshape(b, nblk, WINDOW, C_KV_HEADS, C_GROUP, C_HEAD_DIM)
    kb = k.reshape(b, nblk, WINDOW, C_KV_HEADS, C_HEAD_DIM)
    vb = v.reshape(b, nblk, WINDOW, C_KV_HEADS, C_HEAD_DIM)
    pad = ((0, 0), (1, 0), (0, 0), (0, 0), (0, 0))
    kwin = jnp.concatenate([jnp.pad(kb[:, :-1], pad), kb], axis=2)
    vwin = jnp.concatenate([jnp.pad(vb[:, :-1], pad), vb], axis=2)
    sc = jnp.einsum('bnqcgd,bnkcd->bncgqk', qb, kwin).astype(jnp.float32) * (C_HEAD_DIM ** -0.5)
    qi = jnp.arange(WINDOW)[:, None]
    ki = jnp.arange(2 * WINDOW)[None, :]
    rel = WINDOW + qi - ki
    band = (rel >= 0) & (rel < WINDOW)
    in_seq = (jnp.arange(nblk)[:, None] * WINDOW + jnp.arange(2 * WINDOW)[None, :] - WINDOW) >= 0
    mask = band[None] & in_seq[:, None, :]
    sc = jnp.where(mask[None, :, None, None], sc, -jnp.inf)
    sink = sinks.astype(jnp.float32).reshape(C_KV_HEADS, C_GROUP)[None, None, :, :, None, None]
    m = jnp.maximum(jnp.max(sc, axis=-1, keepdims=True), sink)
    p = jnp.exp(sc - m)
    probs = p / (jnp.sum(p, axis=-1, keepdims=True) + jnp.exp(sink - m))
    o = jnp.einsum('bncgqk,bnkcd->bnqcgd', probs.astype(v.dtype), vwin)
    return o.reshape(b, s, C_HEADS * C_HEAD_DIM) @ w_out

def swiglu_2(h, w_gate, w_up, w_down):
    return (jax.nn.silu(h @ w_gate) * (h @ w_up)) @ w_down

def second_inputs(seed: int = 0) -> dict:
    key = jax.random.key(seed)
    ks = jax.random.split(key, 16)
    f32 = jnp.float32

    def dense(k, shape, fan_in):
        return jax.random.normal(k, shape, f32) * (fan_in ** -0.5)

    x = jax.random.normal(ks[0], (BATCH, SEQ, D_MODEL), f32)
    positions = jnp.broadcast_to(jnp.arange(SEQ, dtype=jnp.int32)[None, :], (BATCH, SEQ))
    norm_gains = 1.0 + 0.02 * jax.random.normal(ks[1], (DEPTH_2, 4, D_MODEL), f32)
    a_w_in = dense(ks[2], (N_A, D_MODEL, A_IN), D_MODEL)
    a_w_out = dense(ks[3], (N_A, A_HEADS * A_V_DIM, D_MODEL), A_HEADS * A_V_DIM)
    a_lambda = 0.1 * jax.random.normal(ks[4], (N_A, 4, A_HEAD_DIM), f32)
    a_subln = 1.0 + 0.02 * jax.random.normal(ks[5], (N_A, A_V_DIM), f32)
    b_w_in = dense(ks[6], (N_B, D_MODEL, B_IN), D_MODEL)
    b_w_out = dense(ks[7], (N_B, B_HEADS * B_HEAD_DIM, D_MODEL), B_HEADS * B_HEAD_DIM)
    c_w_in = dense(ks[8], (N_C, D_MODEL, C_IN), D_MODEL)
    c_w_out = dense(ks[9], (N_C, C_HEADS * C_HEAD_DIM, D_MODEL), C_HEADS * C_HEAD_DIM)
    c_sinks = 0.5 * jax.random.normal(ks[10], (N_C, C_HEADS), f32)
    ffn_w_gate = dense(ks[11], (DEPTH_2, D_MODEL, FFN_HIDDEN), D_MODEL)
    ffn_w_up = dense(ks[12], (DEPTH_2, D_MODEL, FFN_HIDDEN), D_MODEL)
    ffn_w_down = dense(ks[13], (DEPTH_2, FFN_HIDDEN, D_MODEL), FFN_HIDDEN)
    return {"x": x, "positions": positions, "norm_gains": norm_gains,
            "a_w_in": a_w_in, "a_w_out": a_w_out, "a_lambda": a_lambda, "a_subln": a_subln,
            "b_w_in": b_w_in, "b_w_out": b_w_out,
            "c_w_in": c_w_in, "c_w_out": c_w_out, "c_sinks": c_sinks,
            "ffn_w_gate": ffn_w_gate, "ffn_w_up": ffn_w_up, "ffn_w_down": ffn_w_down}

def second_block(x, positions, norm_gains, a_w_in, a_w_out, a_lambda, a_subln,
              b_w_in, b_w_out, c_w_in, c_w_out, c_sinks,
              ffn_w_gate, ffn_w_up, ffn_w_down):
    cos, sin = rope_tables(positions)
    for i in range(DEPTH_2):
        kind = i % N_MIXERS
        inst = i // N_MIXERS
        hn = rms_norm_2(x, norm_gains[i, 0])
        if kind == 0:
            m = diff_attention(hn, a_w_in[inst], a_w_out[inst], a_lambda[inst], a_subln[inst], cos, sin, i)
        elif kind == 1:
            m = stick_breaking_attention(hn, b_w_in[inst], b_w_out[inst])
        else:
            m = sliding_window_sink_attention(hn, c_w_in[inst], c_w_out[inst], c_sinks[inst], cos, sin)
        x = x + rms_norm_2(m, norm_gains[i, 1])
        f = swiglu_2(rms_norm_2(x, norm_gains[i, 2]), ffn_w_gate[i], ffn_w_up[i], ffn_w_down[i])
        x = x + rms_norm_2(f, norm_gains[i, 3])
    return x


def setup_inputs(seed=0):
    out = dict(first_inputs(seed))
    for name, value in second_inputs(seed + 1).items():
        if name != "x":
            out[name + "_2"] = value
    return out


def reference(
    x, c, ada_w, ada_b, norm_g, ffn_w_gate, ffn_w_up, ffn_w_down, hyb_w_in, hyb_w_out,
    lru_conv_w, lru_conv_b, lru_wa, lru_ba, lru_wx, lru_bx, lru_lambda, ssd_conv_w, ssd_conv_b,
    ssd_dt_bias, ssd_a_log, ssd_d, ssd_norm_g, mlstm_w_up, mlstm_conv_w, mlstm_conv_b, mlstm_wq,
    mlstm_wk, mlstm_wv, mlstm_w_gates, mlstm_b_gates, mlstm_norm_g, mlstm_skip, mlstm_w_down,
    final_norm_g, positions_2, norm_gains_2, a_w_in_2, a_w_out_2, a_lambda_2, a_subln_2,
    b_w_in_2, b_w_out_2, c_w_in_2, c_w_out_2, c_sinks_2, ffn_w_gate_2, ffn_w_up_2, ffn_w_down_2,
):
    x = first_block(
        x, c, ada_w, ada_b, norm_g, ffn_w_gate, ffn_w_up, ffn_w_down, hyb_w_in, hyb_w_out,
        lru_conv_w, lru_conv_b, lru_wa, lru_ba, lru_wx, lru_bx, lru_lambda, ssd_conv_w,
        ssd_conv_b, ssd_dt_bias, ssd_a_log, ssd_d, ssd_norm_g, mlstm_w_up, mlstm_conv_w,
        mlstm_conv_b, mlstm_wq, mlstm_wk, mlstm_wv, mlstm_w_gates, mlstm_b_gates, mlstm_norm_g,
        mlstm_skip, mlstm_w_down, final_norm_g,
    )
    return second_block(
        x, positions_2, norm_gains_2, a_w_in_2, a_w_out_2, a_lambda_2, a_subln_2, b_w_in_2,
        b_w_out_2, c_w_in_2, c_w_out_2, c_sinks_2, ffn_w_gate_2, ffn_w_up_2, ffn_w_down_2,
    )


_drawn_inputs = setup_inputs


def setup_inputs(seed=0):
    import zlib

    import numpy as np

    out = dict(_drawn_inputs(seed))
    spreads = {}
    factors = {'lru_ba': 22.84, 'lru_bx': 8.0, 'c_sinks_2': 3.873}
    for name, (base, spread) in spreads.items():
        noise = np.random.default_rng([zlib.crc32(name.encode()), seed]).standard_normal(out[name].shape)
        drawn = base * np.exp(spread * noise) if base else spread * noise
        out[name] = __import__('jax').numpy.asarray(drawn.astype(out[name].dtype))
    for name, factor in factors.items():
        out[name] = (out[name] * factor).astype(out[name].dtype)
    return out
```

```python
from contextlib import ExitStack

import numpy as np

import concourse.bass as bass
from concourse import mybir

F32 = mybir.dt.float32
F32R = mybir.dt.float32r
I32 = mybir.dt.int32
ALU = mybir.AluOpType
ACT = mybir.ActivationFunctionType
AX_X = mybir.AxisListType.X

P = 128
D = 1024
T = 256
KT = D // P
TB = T // P
F = 2816
CHUNKS = F // 256
FIRST_SLOTS = 7
RING = 3
PIECE = 2048
ARENA_F = 17664
EPS = 1e-6
SSD_H, MH = 16, 4
LAM_INIT = [0.8 - 0.6 * float(np.exp(-0.3 * i)) for i in (0, 3)]

PIECES = {"ffn": 3 * CHUNKS, "hyb": 26, "mlstm": 24, "A": 16, "B": 16, "C": 9}
PARTS = {"hyb": 8, "mlstm": 8, "A": 4, "B": 4, "C": 4}
EVACS = {"hyb": 18, "mlstm": 16, "A": 12, "B": 12, "C": 5}
ROTS = {"A": 8, "C": 5}
STAGES = [("ffn", 0), ("hyb", 0), ("ffn", 1), ("ffn", 2), ("mlstm", 0), ("ffn", 3),
          ("A", 0), ("ffn", 4), ("B", 0), ("ffn", 5), ("C", 0), ("ffn", 6), ("A", 1), ("ffn", 7)]
SUB = {("ffn", 0): 0, ("hyb", 0): 1, ("ffn", 1): 2, ("ffn", 2): 3, ("mlstm", 0): 4, ("ffn", 3): 5}
NGAIN = {("A", 0): 0, ("ffn", 4): 2, ("B", 0): 4, ("ffn", 5): 6, ("C", 0): 8, ("ffn", 6): 10,
         ("A", 1): 12, ("ffn", 7): 14}

ROWS = [("norm_g", 48), ("lru_conv_w", 32), ("lru_conv_b", 8), ("lru_ba", 8), ("lru_bx", 8),
        ("lru_lambda", 8), ("ssd_conv_w", 48), ("ssd_conv_b", 12), ("ssd_norm_g", 8),
        ("mlstm_conv_w", 64), ("mlstm_conv_b", 16), ("mlstm_norm_g", 16), ("mlstm_skip", 16),
        ("final_norm_g", 8), ("norm_gains_2", 128), ("ada_b", 144), ("c", 8), ("a_subln_2", 2)]
COL = {}
_n = 0
for _name, _rows in ROWS:
    COL[_name] = _n
    _n += _rows
ROW_TILES = -(-_n // P)
TURN = [6.28125, 1.93500518798828125e-3, float(2 * np.pi - 6.28125 - 1.93500518798828125e-3)]
MAGIC = 1.5 * 2.0 ** 23
ROPE_STEPS = 21
SIZES = dict(ROWS)


def sequence(kind):
    if kind == "B":
        seq = [("in", n) for n in range(6)] + [("unit", 0)]
        for u in range(1, 10):
            seq += ([("in", 5 + u)] if u < 7 else []) + [("unit", u)]
        return seq
    if kind == "A":
        seq = [("in", n) for n in range(6)] + [("rot", 0), ("in", 6), ("rot", 1), ("rot", 2), ("in", 7),
                                               ("unit", 0), ("rot", 3)]
        for u in range(1, 11):
            if u < 5:
                seq += [("in", 7 + u)]
            seq += [("unit", u)]
            if u < 5:
                seq += [("rot", 3 + u)]
        return seq
    seq = [("in", 0), ("in", 1), ("rot", 0), ("in", 2), ("rot", 1), ("in", 3), ("rot", 2), ("unit", 0),
           ("in", 4), ("rot", 3), ("unit", 1), ("rot", 4)]
    return seq + [("unit", u) for u in range(2, 11)]


def mlstm_sequence():
    seq = [("xm", n) for n in range(8)] + [("z", 0), ("gates", 0), ("z", 1), ("cols", 0), ("z", 2), ("a", 0), ("z", 3)]
    after_b, after_d = {0: 4, 1: 5, 2: 6, 3: 7}, {}
    for h in range(MH):
        seq += [("b", h)] + ([("z", after_b[h])] if h in after_b else []) + [("c", h)]
        seq += [("a", h + 1)] if h + 1 < MH else []
        seq += [("d", h)] + ([("z", after_d[h])] if h in after_d else []) + [("e", h)]
    return seq


def hybrid_sequence():
    seq = [("in", 0), ("in", 1), ("lru", 0), ("in", 2), ("lru", 1), ("in", 3), ("lru", 2), ("in", 4), ("lru", 3),
           ("in", 5), ("tanh", 0), ("in", 6), ("exp", 0), ("in", 7), ("sqrt", 0), ("in", 8), ("mix", 0), ("in", 9),
           ("dt", 0), ("in", 10), ("dt", 1), ("in", 11), ("in", 12), ("dt", 2), ("in", 13), ("in", 14),
           ("scan", 0), ("dt", 3), ("cb", 0), ("in", 15), ("y_lru", 0), ("in", 16), ("xs_t", 0), ("in", 17)]
    for u in range(9):
        seq += ([("decay", u)] if u < 8 else []) + ([("row", u // 2 - 1)] if u in (2, 4, 6) else [])
        seq += [("head", u - 1)] if u else []
    return seq + [("norm", 0)] + [("row", c) for c in range(3, 8)]


class Plan:

    def __init__(self, stages):
        self.steps = []
        n = sq = norm = up = parts = evac = rots = 0
        for k, key in enumerate(stages):
            second = key in NGAIN
            self.steps.append(dict(key=key, piece=n, sq=sq, norm=norm, down=norm, up=up, second=second,
                                   ffn=sum(s[0] == "ffn" for s in stages[:k]),
                                   parts=parts, evac=evac, rots=rots,
                                   att=8 * sum(s[0] in "ABC" for s in stages[:k]),
                                   soft=8 * sum(s[0] in "AC" for s in stages[:k]),
                                   soft_a=4 * sum(s[0] == "A" for s in stages[:k])))
            n += PIECES[key[0]]
            parts += PARTS.get(key[0], 0)
            evac += EVACS.get(key[0], 0)
            rots += ROTS.get(key[0], 0)
            sq += 2 if second else 1
            norm += 1
            up += 1
            if key == ("ffn", 3):
                sq += 1
                up += 1
        self.pieces = n
        self.updates = up
        self.subs = [SUB[s] for s in stages if s in SUB]


def build(nc, a, out, stages):
    plan = Plan(stages)
    NP = plan.pieces
    later_subs = plan.subs[1:]
    with ExitStack() as ctx:
        def sb(name, shape, dt=F32):
            return ctx.enter_context(nc.sbuf_tensor(name, shape, dt))

        def sem(name):
            return ctx.enter_context(nc.semaphore(name))

        w_raw = sb("w_raw", [P, RING, PIECE])
        w_hi = sb("w_hi", [P, RING, PIECE], F32R)
        w_lo = sb("w_lo", [P, RING, PIECE], F32R)
        ada_w = sb("ada_wbuf", [P, KT, 256])
        ada_acc = sb("ada_acc", [P, 24 * P])
        XT = sb("XT", [P, KT, T])
        work = sb("work", [P, KT, T])
        h_hi = sb("h_hi", [P, KT, T], F32R)
        h_lo = sb("h_lo", [P, KT, T], F32R)
        d_hi = sb("d_hi", [P, 2, 2, T], F32R)
        d_lo = sb("d_lo", [P, 2, 2, T], F32R)
        gate_s = sb("gate_s", [P, 2, T])
        hid = sb("hid", [P, 2, T])
        lnb = sb("lnb", [P, T])
        rstd = sb("rstd", [P, T])
        cols = sb("cols", [P, ROW_TILES * P])
        mods = sb("mods", [P, 6, 24])
        c_act = sb("c_act", [P, KT])
        ident = sb("ident", [P, P])
        ones = sb("ones", [P, P])
        eps_c = sb("eps_c", [P, 1])
        sub_mark = sb("sub_mark", [P, 1])
        scrap = sb("scrap", [P, 1])
        causal = sb("causal", [P, 384])
        strict = sb("strict", [P, 384])
        later = sb("later", [P, P])
        turn = sb("turn", [P, P])
        cos_t = sb("cos_t", [P, T])
        sin_t = sb("sin_t", [P, T])
        a_mask = sb("a_mask", [P, 384])
        c_mask = sb("c_mask", [P, 384])
        sinks = sb("sinks", [P, 16])
        lam = sb("lam", [P, 2])
        blocks = sb("blocks", [P, 32])
        sub_g = sb("sub_g", [P, 2])
        inv_freq = sb("inv_freq", [P, 1])
        ARENA = sb("ARENA", [P, ARENA_F])

        def arena(off, *shape):
            size = int(np.prod(shape))
            assert off + size <= ARENA_F, (off, shape)
            v = ARENA[:, off:off + size]
            if len(shape) == 2:
                v = v.rearrange("p (a b) -> p a b", a=shape[0])
            elif len(shape) == 3:
                v = v.rearrange("p (a b c) -> p a b c", a=shape[0], b=shape[1])
            return v

        PS = [ctx.enter_context(nc.psum_tensor(f"bank{i}", [P, 512], F32)) for i in range(8)]
        IO = PS[4:7]
        MISC = PS[7]

        def acc(m):
            return PS[m // 2][:, (m % 2) * T:(m % 2 + 1) * T]

        def accp(j):
            return PS[j][:, :]

        def io(n):
            return IO[n % RING][:, :].rearrange("p (t n) -> p t n", t=2)

        def col(name, i):
            return cols[:, COL[name] + i:COL[name] + i + 1]

        raw_loaded = [sem(f"raw_loaded{s}") for s in range(RING)]
        hi_ready = sem("hi_ready")
        lo_ready = sem("lo_ready")
        piece_used = sem("piece_used")
        sq_ready = sem("sq_ready")
        ss_ready = sem("ss_ready")
        rstd_ready = sem("rstd_ready")
        t_ready = sem("t_ready")
        hhi_ready = sem("hhi_ready")
        hlo_ready = sem("hlo_ready")
        xt_ready = sem("xt_ready")
        acc_done = sem("acc_done")
        silu_ready = sem("silu_ready")
        hid_full = sem("hid_full")
        hid_ready = sem("hid_ready")
        dve_chain = sem("dve_chain")
        act_chain = sem("act_chain")
        pool_chain = sem("pool_chain")
        const_ready = sem("const_ready")
        in_loaded = sem("in_loaded")
        x_loaded = sem("x_loaded")
        first_loaded = [sem(f"first_loaded{s}") for s in range(FIRST_SLOTS)]
        first_copied = sem("first_copied")
        first_cols = sem("first_cols")
        gate_sub = sem("gate_sub")
        gate_sum = sem("gate_sum")
        gate_loaded = sem("gate_loaded")
        gate_dve = sem("gate_dve")
        first_used = sem("first_used")
        rowsT = sem("rowsT")
        cols_ready = sem("cols_ready")
        c_ready = sem("c_ready")
        xin_T = sem("xin_T")
        ada_loaded = [sem(f"ada_loaded{x}") for x in range(2)]
        ada_sub = sem("ada_sub")
        mod_sum = sem("mod_sum")
        mod_ready = sem("mod_ready")
        outT = sem("outT")
        out_ready = sem("out_ready")
        stored = sem("stored")

        first_w = arena(0, FIRST_SLOTS, PIECE)
        x_in = work[:, :, :].rearrange("p k n -> p (k n)").rearrange("p (b d) -> p b d", b=TB)
        rows_in = arena(16784, ROW_TILES, P)
        gate_acc = arena(0, 8 * P)
        first_row = arena(PIECE, PIECE)[0:1, :]
        out_sb = arena(0, TB, D)

        def bank_summed(eng, st, j):
            if j < 3:
                eng.wait_ge(acc_done, 3 * st["down"] + j + 1)
            else:
                eng.wait_ge(piece_used, st["piece"] + PIECES[st["key"][0]])

        masks_ready = sem("masks_ready")
        (m_loaded, m_conv, m_xc, m_bd, m_bd_used, m_gsb, m_gates, m_rows, m_rowd, m_colT, m_qk, m_qks, m_vs, m_s,
         m_mb, m_e, m_ex, m_w, m_den, m_num, m_absd, m_hh, m_mean, m_hc, m_sq, m_var, m_rs, m_y) = (
            sem(f"mlstm_{n}") for n in ("loaded", "conv", "xc", "blocks", "blocks_used", "gate_weights", "gates",
                                        "rows_act", "rows_dve", "columns", "qk", "qk_copied", "v_copied", "scores",
                                        "rows_spread", "exponent", "decay", "weights", "den", "num", "den_read",
                                        "h", "mean", "centred", "squares", "var", "rstd", "y"))
        small_loaded = sem("small_loaded")
        rope_chain = sem("rope_chain")
        rope_ready = sem("rope_ready")
        lam_ready = sem("lam_ready")
        parts_ready = sem("parts_ready")
        proj_ready = sem("proj_ready")
        turned = sem("turned")
        roped = sem("roped")
        s_ready = sem("s_ready")
        ot_ready = sem("ot_ready")
        o_ready = sem("o_ready")
        ln_ready = sem("ln_ready")
        sp_ready = sem("sp_ready")
        nb_ready = sem("nb_ready")
        spm_ready = sem("spm_ready")
        r_ready = sem("r_ready")
        arg_ready = sem("arg_ready")
        e_ready = sem("e_ready")
        a_ready = sem("a_ready")
        negm_ready = sem("negm_ready")
        p_ready = sem("p_ready")
        w_ready = sem("w_ready")
        wT_ready = sem("wT_ready")
        wTs_ready = sem("wTs_ready")
        vdup_ready = sem("vdup_ready")
        sub_sq = sem("sub_sq")
        sub_sum = sem("sub_sum")
        sub_rstd = sem("sub_rstd")
        sub_ln = sem("sub_ln")

        V = arena(0, TB, D)
        Q = arena(2048, KT, T)
        K = arena(4096, KT, T)
        OT = arena(6144, KT, T)
        raw_qk = arena(8192, 2, 2, T)
        rot_a = arena(9216, 2, T)
        rot_b = arena(9728, 2, T)
        lnv = arena(10240, 2, 384)
        sp = arena(11008, 2, 384)
        nb = arena(11776, 2, 2, 384)
        sc = arena(10240, 2, 384)
        pr_of = [arena(11008, 2, 384), arena(16784, 2, 384)]
        wts = arena(11776, 2, 384)
        wT = arena(12544, 2, 384)
        KD = arena(13312, 2, T)
        VD = arena(13824, TB, 2, P)
        osq = arena(4096, KT, T)
        osl = arena(2048, KT, T)
        stat_of = [arena(14336, 16), arena(14352, 16)]
        rope_w = [arena(14400 + 256 * k, T) for k in range(6)]
        lam_w = arena(16000, 2, 4, 64)
        lam_p = arena(16512, 2, 2, 64)
        lam_s = arena(16768, 8)
        pos_i = sb("pos_i", [P, T], I32)

        XM = arena(0, 16, T + 3)
        XC = arena(4144, 16, T)
        ZS = arena(8240, 16, T)
        QK = arena(12336, 4, 2 * T)
        VH = arena(14384, TB, 512)
        GE = arena(15408, 32, 36)
        BD = arena(16560, 2, 3, P)
        c_col = arena(17328, 8)
        b_gate = arena(17336, 2)
        WG = arena(12336, 48, 36)
        wf = work[:, :, :].rearrange("p k n -> p (k n)")
        w4 = wf[:, 1536:1920].rearrange("p (k t o) -> p k t o", k=6, t=16)
        f_row, i_row, ln_row, b_row, m_row, em_row = (wf[0:MH, 256 * k:256 * k + 256] for k in range(6))
        xm_in = XM[:, :, 3:T + 3]
        gate_f = gate_s[:, :, :].rearrange("p a b -> p (a b)")
        hid_f = hid[:, :, :].rearrange("p a b -> p (a b)")
        EW, WW = gate_f[:, 0:384], hid_f[:, 0:384]

        XR = arena(0, 8, T + 3)
        XL = arena(2072, KT, T)
        GL = arena(4120, KT, T)
        TI = arena(6168, KT, T)
        XC_T = arena(6168, TB, D)
        WAX = arena(8216, 2, 8, P)
        BCR = arena(10264, 4, T + 3)
        BC = arena(11300, 4, T)
        XS = arena(12324, KT, T)
        ZG = arena(14372, KT, T)
        RC = arena(14372, KT, T)
        CB = arena(16420, 2, 384)
        small_h = arena(17188, 168)
        w_dt = small_h[:, 0:128].rearrange("p (k h) -> p k h", k=KT)
        d_col, dt_bias, a_log = small_h[:, 128:136], small_h[:, 136:152], small_h[:, 152:168]
        dt = arena(17356, TB, 16)
        dta = arena(17388, TB, 16)
        acs_c = arena(17420, TB, 16)
        sp_lam, lam_4, lam_2 = arena(17452, 8), arena(17460, 8), arena(17468, 8)
        dt_ln = arena(17476, TB, 16)
        acs_r = rstd[0:SSD_H, :]
        hyb_rs = gate_s

        def decay_of(u):
            return arena(8216 + 768 * (u % 2), 2, 384)

        (y_loaded, y_lam, y_lam_ln, y_conv, y_gates, y_th, y_decay, y_mix, y_scan, y_bc_conv, y_bc, y_cb, y_cb_read,
         y_xs_conv, y_xs, y_xst, y_xc, y_dt, y_dt_raw, y_dt_ln, y_dta, y_dt_r, y_acs, y_r, y_e, y_ex, y_w, y_o, y_y,
         y_sq, y_sum, y_rs, y_ssd) = (
            sem(f"hybrid_{n}") for n in ("loaded", "lambda", "lambda_ln", "conv", "gates", "gates_read", "decays",
                                         "scan_input", "lru_out", "bc_conv", "bc", "cb", "cb_read", "xs_conv", "xs",
                                         "xs_turned", "xc", "dt_sums", "dt_biased", "dt_ln", "dta", "dt_pe", "acs",
                                         "rows_spread", "exponent", "decay", "weights", "out", "y", "squares",
                                         "sums", "rstd", "ssd_out"))
        block = ctx.enter_context(nc.Block())

        @block.sync
        def _(sp):
            sp.dma_start(rows_in, a["rows"]).then_inc(in_loaded, 16)
            for n in range(2):
                if plan.subs:
                    sp.dma_start(first_w[:, n, :], a["ada"][12 * plan.subs[0] + n]).then_inc(first_loaded[n], 16)
            sp.dma_start(inv_freq[:, :], a["inv_freq"]).then_inc(small_loaded, 16)
            sp.dma_start(pos_i[:, :], a["positions"].partition_broadcast(P)).then_inc(small_loaded, 16)
            sp.dma_start(sinks[:, :], a["sinks"].partition_broadcast(P)).then_inc(small_loaded, 16)
            sp.dma_start(lam_w[:, :, :, :].rearrange("p a b c -> p (a b c)"),
                         a["lambda"].partition_broadcast(P)).then_inc(small_loaded, 16)
            for n in range(2, FIRST_SLOTS):
                if plan.subs:
                    sp.dma_start(first_w[:, n, :], a["ada"][12 * plan.subs[0] + n]).then_inc(first_loaded[n], 16)
                if n == 3:
                    sp.dma_start(x_in, a["x"].rearrange("(b p) d -> p b d", p=P)).then_inc(x_loaded, 16)
            if plan.subs:
                for n in range(FIRST_SLOTS, 8):
                    sp.wait_ge(first_used, n - FIRST_SLOTS + 1)
                    m = n % FIRST_SLOTS
                    sp.dma_start(first_w[:, m, :], a["ada"][12 * plan.subs[0] + n]).then_inc(first_loaded[m], 16)
            for n in range(RING):
                sp.dma_start(w_raw[:, n, :], a["ws"][n]).then_inc(raw_loaded[n], 16)
            if plan.subs:
                sp.wait_ge(first_used, 8)
                for n in range(2):
                    sp.dma_start(first_w[:, 3 + n, :], a["ada"][12 * plan.subs[0] + 8 + n]).then_inc(gate_loaded, 16)
            with sp.Fori(1, NP // RING) as r:
                for s in range(RING):
                    sp.wait_ge(lo_ready, r * RING + (s - RING + 1))
                    sp.dma_start(w_raw[:, s, :], a["ws"][r * RING + s]).then_inc(raw_loaded[s], 16)
            for n in range(NP // RING * RING, NP):
                sp.wait_ge(lo_ready, n - RING + 1)
                sp.dma_start(w_raw[:, n % RING, :], a["ws"][n]).then_inc(raw_loaded[n % RING], 16)
            for b in range(TB):
                sp.wait_ge(out_ready, 2 * b + 2)
                sp.dma_start(out[b * P:(b + 1) * P, :], out_sb[:, b, :]).then_inc(stored, 16)
            sp.wait_ge(stored, 16 * TB)

        @block.gpsimd
        def _(pool):
            nchain = [0]

            def link(ins):
                nchain[0] += 1
                ins.then_inc(pool_chain, 1)
                pool.wait_ge(pool_chain, nchain[0])

            link(pool.memset(ident[:, :], 0.0))
            pool.memset(ones[:, :], 1.0).then_inc(const_ready, 1)
            pool.memset(eps_c[:, :], EPS).then_inc(const_ready, 1)
            pool.affine_select(out=ident[:, :], in_=ident[:, :], compare_op=ALU.not_equal, fill=1.0, base=0,
                               pattern=[[-1, P]], channel_multiplier=1).then_inc(const_ready, 1)
            for t in (causal, strict, later):
                link(pool.memset(t[:, :], 1.0))
            for t in (turn, a_mask, c_mask):
                link(pool.memset(t[:, :], 0.0))
            halves = turn[:, :].rearrange("p (h c) -> p h c", h=2)

            def keep(view, op, fill, base, pattern, multiplier):
                link(pool.affine_select(out=view, in_=view, compare_op=op, fill=fill, base=base,
                                        pattern=pattern, channel_multiplier=multiplier))

            keep(causal[:, 0:256], ALU.is_ge, 0.0, 0, [[1, 256]], -1)
            keep(causal[:, 256:384], ALU.is_ge, 0.0, 0, [[1, P]], -1)
            keep(strict[:, 0:256], ALU.is_gt, 0.0, 0, [[1, 256]], -1)
            keep(strict[:, 256:384], ALU.is_gt, 0.0, 0, [[1, P]], -1)
            keep(later[:, :], ALU.is_gt, 0.0, 0, [[-1, P]], 1)
            keep(halves[:, :, 0:32], ALU.not_equal, -1.0, -32, [[-64, 2], [-1, 32]], 1)
            keep(halves[:, :, 32:64], ALU.not_equal, 1.0, 0, [[-64, 2], [-1, 32]], 1)
            keep(a_mask[:, 0:256], ALU.is_ge, -1e30, 128, [[-1, 256]], 1)
            keep(a_mask[:, 256:384], ALU.is_ge, -1e30, 0, [[-1, P]], 1)
            keep(c_mask[:, 0:128], ALU.is_gt, -1e30, 0, [[1, P]], -1)
            keep(c_mask[:, 128:256], ALU.is_ge, -1e30, 0, [[-1, P]], 1)
            keep(c_mask[:, 256:384], ALU.is_ge, -1e30, 0, [[-1, P]], 1)
            link(pool.memset(blocks[:, :], 1.0))
            keep(blocks[:, :], ALU.is_ge, 0.0, 0, [[-4, 32]], 1)
            keep(blocks[:, :], ALU.is_ge, 0.0, 3, [[4, 32]], -1)
            pool.memset(sub_mark[:, :], 0.0).then_inc(masks_ready, 1)
            cb = c_act[:, :].unsqueeze(2).broadcast_to([P, KT, 256])
            loads = [0]

            def modulation_sums(piece0, pieces, dst):
                base, loaded = nchain[0], loads[0]
                half = [ada_w[:, 4 * x:4 * x + 4, :] for x in range(2)]

                def load(x, i):
                    pool.dma_start(half[x].rearrange("p k n -> p (k n)"),
                                   a["ada"][i + piece0, :, x * 1024:(x + 1) * 1024]).then_inc(ada_loaded[x], 16)

                def step(i, more):
                    for x in range(2):
                        pool.wait_ge(ada_loaded[x], i * 16 + (loaded + 1) * 16)
                        pool.tensor_tensor(half[x], half[x], cb[:, 4 * x:4 * x + 4, :], ALU.mult).then_inc(pool_chain, 1)
                    pool.wait_ge(pool_chain, i * 5 + base + 2)
                    pool.tensor_tensor(half[1], half[1], half[0], ALU.add).then_inc(pool_chain, 1)
                    pool.wait_ge(pool_chain, i * 5 + base + 3)
                    if more:
                        load(0, i + 1)
                    pool.tensor_tensor(ada_w[:, 4:6, :], ada_w[:, 4:6, :], ada_w[:, 6:8, :],
                                       ALU.add).then_inc(pool_chain, 1)
                    pool.wait_ge(pool_chain, i * 5 + base + 4)
                    pool.tensor_tensor(dst[:, bass.ts(i, 256)], ada_w[:, 4, :], ada_w[:, 5, :],
                                       ALU.add).then_inc(pool_chain, 1)
                    pool.wait_ge(pool_chain, i * 5 + base + 5)
                    if more:
                        load(1, i + 1)

                load(0, 0)
                load(1, 0)
                with pool.Fori(0, pieces - 1) as i:
                    step(i, True)
                step(pieces - 1, False)
                nchain[0] += 5 * pieces
                loads[0] += pieces

            def first_gate():
                pool.wait_ge(first_used, 8)
                modulation_sums(12 * plan.subs[0] + 10, 2, gate_acc[:, 512:1024])
                pool.memset(sub_mark[:, :], 0.0).then_inc(gate_sub, 1)

            if plan.subs:
                pool.wait_ge(c_ready, 1)
            for k, s in enumerate(later_subs):
                if k:
                    pool.wait_ge(mod_sum, k)
                modulation_sums(12 * s, 12, ada_acc)
                pool.memset(sub_mark[:, :], 0.0).then_inc(ada_sub, 1)
                if k == 0:
                    first_gate()
            if plan.subs and not later_subs:
                first_gate()

            both = strict[:, :].unsqueeze(1).broadcast_to([P, 2, 384])
            for st in plan.steps:
                if st["key"][0] == "B":
                    for kind, u in sequence("B"):
                        if kind != "unit":
                            continue
                        if u < 8:
                            pool.wait_ge(sp_ready, u + 1)
                            pool.tensor_tensor(sp, sp, both, ALU.mult).then_inc(spm_ready, 1)

        @block.scalar
        def _(act):
            nchain = [0]

            def link(ins):
                nchain[0] += 1
                ins.then_inc(act_chain, 1)

            def chained():
                act.wait_ge(act_chain, nchain[0])

            def hi(n, slot, loads):
                act.wait_ge(raw_loaded[slot], loads)
                act.wait_ge(piece_used, n - RING + 1) if not (type(n) is int and n < RING) else None
                act.activation(w_hi[:, slot, :], w_raw[:, slot, :], ACT.Copy).then_inc(hi_ready, 1)

            def hi_ahead(n0, i=None):
                if n0 >= NP:
                    return
                if i is None:
                    hi(n0, n0 % RING, 16 * (n0 // RING + 1))
                else:
                    hi(i * RING + n0, n0 % RING, i * 16 + 16 * (n0 // RING + 1))

            def squares(e, src, ready):
                for j in range(4):
                    ready(j)
                    act.activation(work[:, 2 * j:2 * j + 2, :], src(j), ACT.Square).then_inc(sq_ready, 1)

            def inv_rms(e):
                act.activation(scrap[:, :], ones[:, 0:1], ACT.Ln)
                act.wait_ge(ss_ready, e + 1)
                link(act.activation(lnb[:, :], MISC[:, 0:T], ACT.Ln, bias=eps_c[:, 0:1], scale=1.0 / D))
                chained()
                act.activation(rstd[:, :], lnb[:, :], ACT.Exp, scale=-0.5).then_inc(rstd_ready, 1)

            def xt_pair(j):
                return XT[:, 2 * j:2 * j + 2, :]

            def acc_pair(j):
                return accp(j).rearrange("p (t n) -> p t n", t=2)

            def normalise(st):
                if st is plan.steps[0]:
                    act.wait_ge(xin_T, 4)
                squares(st["sq"], xt_pair, lambda j: act.wait_ge(xt_ready, 8 * st["up"] + 2 * j + 2))
                if st is plan.steps[0]:
                    for n in range(2):
                        hi_ahead(n)
                inv_rms(st["sq"])
                for kt in range(KT):
                    act.wait_ge(t_ready, 8 * st["norm"] + kt + 1)
                    if st["second"]:
                        ins = act.activation(h_hi[:, kt, :], work[:, kt, :], ACT.Copy)
                    else:
                        ins = act.activation(h_hi[:, kt, :], work[:, kt, :], ACT.Identity,
                                             bias=mods[:, SUB[st["key"]], kt:kt + 1])
                    ins.then_inc(hhi_ready, 1)

            def finish_update(st):
                if st["second"]:
                    e = st["sq"] + 1
                    squares(e, acc_pair, lambda j: bank_summed(act, st, j))
                    inv_rms(e)

            def final_norm(st):
                e = st["sq"] + 1
                squares(e, xt_pair, lambda j: act.wait_ge(xt_ready, 8 * st["up"] + 2 * j + 10))
                inv_rms(e)

            def ffn(st):
                n, c0 = st["piece"], CHUNKS * st["ffn"]
                normalise(st)
                hi_ahead(n + 2)
                act.wait_ge(piece_used, n + 1)
                if c0:
                    act.wait_ge(hid_full, c0)
                act.activation(gate_s[:, :, :], io(n), ACT.Silu).then_inc(silu_ready, 1)
                hi_ahead(n + 3)

                def body(n0, i, c):
                    hi_ahead(n0 + 2, i)
                    g = n0 if i is None else i * RING + n0
                    act.wait_ge(piece_used, g + 1)
                    act.wait_ge(hid_full, c)
                    act.activation(gate_s[:, :, :], io(n0), ACT.Silu).then_inc(silu_ready, 1)
                    hi_ahead(n0 + 3, i)
                    hi_ahead(n0 + 4, i)

                body(n + 2, None, c0 + 1)
                with act.Fori(1, CHUNKS - 2) as i:
                    body(n + 2, i, i + (c0 + 1))
                body(n + 2 + RING * (CHUNKS - 2), None, c0 + CHUNKS - 1)
                hi_ahead(n + 3 * CHUNKS - 1 + 2)
                finish_update(st)

            def evacuate(st, i):
                kind, n = st["key"][0], st["piece"] + i
                act.wait_ge(piece_used, n + 1)
                b = io(n)
                if kind == "C" and i == 0:
                    act.activation(raw_qk[:, 0, 0, :], b[:, 0, :], ACT.Copy)
                    v = b[:, 1, :].rearrange("p (b c) -> p b c", b=TB)
                    for m in range(2):
                        for k in range(2):
                            ins = act.activation(VD[:, :, m, 64 * k:64 * k + 64], v[:, :, 64 * m:64 * m + 64], ACT.Copy)
                    ins.then_inc(proj_ready, 1)
                    return
                if kind != "C" and i < 4:
                    act.activation(V[:, :, 256 * i:256 * i + 256], b, ACT.Copy).then_inc(proj_ready, 1)
                    return
                query = kind == "C" or i % 2 == 0
                if kind == "B":
                    j = i // 2 - 2
                    dst = (Q if query else K)[:, 2 * j:2 * j + 2, :]
                else:
                    rot = i if kind == "C" else i - 4
                    if rot >= 2:
                        act.wait_ge(roped, st["rots"] + rot - 1)
                    dst = raw_qk[:, rot % 2, :, :]
                act.activation(dst, b, ACT.Copy, scale=0.125 if query else 1.0).then_inc(proj_ready, 1)

            def outputs(st, u):
                act.wait_ge(o_ready, st["att"] + u + 1)
                if st["key"][0] == "A":
                    act.activation(OT[:, u, :], MISC[:, 0:T], ACT.Copy).then_inc(ot_ready, 1)
                else:
                    act.activation(OT[0:64, u, :], MISC[0:64, 0:T], ACT.Copy)
                    act.activation(OT[64:128, u, :], MISC[64:128, T:2 * T], ACT.Copy).then_inc(ot_ready, 1)

            def stick_unit(st, u):
                if u < 8:
                    act.wait_ge(s_ready, st["att"] + u + 1)
                    if u:
                        act.wait_ge(nb_ready, u)
                    for h in range(2):
                        link(act.activation(lnv[:, h, :], PS[h][:, 0:384], ACT.Abs))
                    chained()
                    link(act.activation(lnv, lnv, ACT.Exp, scale=-1.0))
                    chained()
                    act.activation(lnv, lnv, ACT.Ln, bias=ones[:, 0:1]).then_inc(ln_ready, 1)
                if 1 <= u < 9:
                    act.wait_ge(arg_ready, u)
                    w = nb[:, (u - 1) % 2, :, :]
                    act.activation(w, w, ACT.Exp).then_inc(e_ready, 1)
                if u >= 2:
                    outputs(st, u - 2)

            def soft_unit(st, u):
                nh = 1 if st["key"][0] == "A" else 2
                if u < 8:
                    pr, stat = pr_of[u % 2], stat_of[u % 2]
                    act.wait_ge(negm_ready, st["soft"] + u + 1)
                    if u >= 2:
                        act.wait_ge(w_ready, st["soft"] + u - 1)
                    if st["key"][0] == "C":
                        act.activation(stat[:, 12:16], stat[:, 12:16], ACT.Exp)
                    for k, (lo_c, hi_c) in enumerate(((0, 256), (256, 384))):
                        for h in range(2):
                            ins = act.activation(pr[:, h, lo_c:hi_c], sc[:, h, lo_c:hi_c], ACT.Exp,
                                                 bias=stat[:, 4 + 2 * k + h:5 + 2 * k + h],
                                                 accum_out=stat[:, 8 + 2 * k + h:9 + 2 * k + h])
                    ins.then_inc(p_ready, 1)
                if 2 <= u < 10:
                    act.wait_ge(wT_ready, st["soft"] + u - 1)
                    if u >= 3:
                        act.wait_ge(o_ready, st["att"] + u - 2)
                    for h in range(nh):
                        ins = act.activation(wT[:, h, :], PS[2 + h][:, 0:384], ACT.Copy)
                    ins.then_inc(wTs_ready, 1)
                if u >= 3:
                    outputs(st, u - 3)

            def head_norm(st):
                for j in range(4):
                    act.wait_ge(ot_ready, st["att"] + 2 * j + 2)
                    act.activation(osq[:, 2 * j:2 * j + 2, :], OT[:, 2 * j:2 * j + 2, :], ACT.Square).then_inc(sub_sq, 1)
                for j in range(4):
                    act.wait_ge(sub_sum, st["soft_a"] + j + 1)
                    act.activation(osl[:, 2 * j:2 * j + 2, :], acc_pair(j), ACT.Ln, bias=eps_c[:, 0:1],
                                   scale=1.0 / P).then_inc(sub_ln, 1)
                for j in range(4):
                    act.wait_ge(sub_ln, st["soft_a"] + j + 1)
                    v = osl[:, 2 * j:2 * j + 2, :]
                    act.activation(v, v, ACT.Exp, scale=-0.5).then_inc(sub_rstd, 1)

            def attention(st):
                kind, n0 = st["key"][0], st["piece"]
                normalise(st)
                for step, k in sequence(kind):
                    if step == "in":
                        hi_ahead(n0 + k + 2)
                        evacuate(st, k)
                    elif step == "unit":
                        (stick_unit if kind == "B" else soft_unit)(st, k)
                if kind == "A":
                    head_norm(st)
                for k in range(PIECES[kind] - 4, PIECES[kind]):
                    hi_ahead(n0 + k + 2)
                finish_update(st)

            def hybrid(st):
                n0 = st["piece"]
                normalise(st)
                act.wait_ge(hlo_ready, 8 * st["norm"] + 8)
                act.dma_start(WAX.rearrange("p w t o -> p (w t o)"), a["wax"]).then_inc(y_loaded, 16)
                act.dma_start(small_h, a["small_h"]).then_inc(y_loaded, 16)
                link(act.activation(sp_lam, cols[:, COL["lru_lambda"]:COL["lru_lambda"] + 8], ACT.Abs))
                chained()
                link(act.activation(sp_lam, sp_lam, ACT.Exp, scale=-1.0))
                chained()
                act.activation(sp_lam, sp_lam, ACT.Ln, bias=ones[:, 0:1]).then_inc(y_lam_ln, 1)
                for step, k in hybrid_sequence():
                    if step == "in":
                        hi_ahead(n0 + k + 2)
                        act.wait_ge(piece_used, n0 + k + 1)
                        b = io(n0 + k)
                        if k < 4:
                            act.activation(XR[:, 2 * k:2 * k + 2, 3:T + 3], b, ACT.Copy).then_inc(proj_ready, 1)
                        elif k < 8:
                            act.activation(GL[:, 2 * k - 8:2 * k - 6, :], b, ACT.Gelu_apprx_tanh).then_inc(proj_ready, 1)
                        elif k < 10:
                            j = 2 * (k - 8)
                            act.activation(BCR[:, j:j + 2, 3:T + 3], b, ACT.Copy).then_inc(proj_ready, 1)
                        elif k < 14:
                            act.wait_ge(y_conv, 4)
                            j = 2 * (k - 10)
                            act.activation(XR[:, j:j + 2, 3:T + 3], b, ACT.Copy).then_inc(proj_ready, 1)
                        else:
                            act.wait_ge(y_mix, 1)
                            j = 2 * (k - 14)
                            act.activation(ZG[:, j:j + 2, :], b, ACT.Silu).then_inc(proj_ready, 1)
                        if k == 10:
                            for j in range(2):
                                act.wait_ge(y_bc_conv, j + 1)
                                for t in (2 * j, 2 * j + 1):
                                    ins = act.activation(BC[:, t, :], BC[:, t, :], ACT.Silu, bias=col("ssd_conv_b", 8 + t))
                                ins.then_inc(y_bc, 1)
                        if 11 <= k < 15:
                            j = k - 11
                            act.wait_ge(y_xs_conv, j + 1)
                            for t in (2 * j, 2 * j + 1):
                                ins = act.activation(XS[:, t, :], XS[:, t, :], ACT.Silu, bias=col("ssd_conv_b", t))
                            ins.then_inc(y_xs, 1)
                    elif step == "row":
                        hi_ahead(n0 + 18 + k + 2)
                    elif step == "lru":
                        if k == 0:
                            act.wait_ge(y_lam, 1)
                        for t in (2 * k, 2 * k + 1):
                            act.wait_ge(y_gates, t + 1)
                            act.activation(work[:, t, :], PS[t % 4][:, 0:T], ACT.Tanh, bias=col("lru_ba", t), scale=0.5)
                            act.activation(TI[:, t, :], PS[t % 4][:, T:2 * T], ACT.Tanh, bias=col("lru_bx", t),
                                           scale=0.5).then_inc(y_th, 1)
                    elif step == "tanh":
                        act.wait_ge(y_th, 8)
                        for t in range(KT):
                            link(act.activation(RC[:, t, :], work[:, t, :], ACT.Tanh, bias=lam_4[:, t:t + 1],
                                                scale=lam_4[:, t:t + 1]))
                    elif step == "exp":
                        chained()
                        for t in range(KT):
                            link(act.activation(work[:, t, :], work[:, t, :], ACT.Exp, bias=lam_2[:, t:t + 1],
                                                scale=lam_2[:, t:t + 1]))
                    elif step == "sqrt":
                        chained()
                        act.activation(RC, RC, ACT.Sqrt, scale=-1.0).then_inc(y_decay, 1)
                    elif step == "dt":
                        if k == 0:
                            act.wait_ge(y_dt_raw, 1)
                            link(act.activation(dt_ln, dt, ACT.Abs))
                            chained()
                            link(act.activation(dt_ln, dt_ln, ACT.Exp, scale=-1.0))
                            chained()
                            link(act.activation(dt_ln, dt_ln, ACT.Ln, bias=ones[:, 0:1]))
                            chained()
                            act.activation(a_log, a_log, ACT.Exp).then_inc(y_dt_ln, 1)
                        elif k == 2:
                            act.wait_ge(y_dt_r, 1)
                            act.activation(acs_r, MISC[0:SSD_H, 0:T], ACT.Copy).then_inc(y_acs, 1)
                        elif k == 3:
                            act.wait_ge(y_dt_r, 2)
                            act.activation(acs_c, MISC[:, 288:320].rearrange("p (b h) -> p b h", b=TB),
                                           ACT.Copy).then_inc(y_acs, 1)
                    elif step == "decay":
                        act.wait_ge(y_e, k + 1)
                        act.activation(decay_of(k), decay_of(k), ACT.Exp).then_inc(y_ex, 1)
                    elif step == "norm":
                        act.wait_ge(y_scan, 1)
                        for g in range(2):
                            act.wait_ge(y_y, 4 * g + 4)
                            act.activation(work[:, 4 * g:4 * g + 4, :], ZG[:, 4 * g:4 * g + 4, :],
                                           ACT.Square).then_inc(y_sq, 1)
                        act.wait_ge(y_sum, 1)
                        link(act.activation(hyb_rs[:, :, :], MISC[:, :].rearrange("p (g n) -> p g n", g=2), ACT.Ln,
                                            bias=eps_c[:, 0:1], scale=1.0 / 512))
                        chained()
                        act.activation(hyb_rs[:, :, :], hyb_rs[:, :, :], ACT.Exp, scale=-0.5).then_inc(y_rs, 1)
                finish_update(st)

            def mlstm(st):
                n0 = st["piece"]
                normalise(st)
                act.wait_ge(hlo_ready, 8 * st["norm"] + 8)
                act.dma_start(wf[:, 1536:1920], a["w4"]).then_inc(m_loaded, 16)
                act.dma_start(WG.rearrange("p t g -> p (t g)"), a["wg"]).then_inc(m_loaded, 16)
                act.dma_start(b_gate[0:MH, :], a["b_gate"]).then_inc(m_loaded, 16)

                def conv_silu(i):
                    act.wait_ge(m_conv, i + 1)
                    for t in (2 * i, 2 * i + 1):
                        ins = act.activation(XC[:, t, :], XC[:, t, :], ACT.Silu, bias=col("mlstm_conv_b", t))
                    ins.then_inc(m_xc, 1)

                for step, k in mlstm_sequence():
                    if step == "xm":
                        hi_ahead(n0 + k + 2)
                        act.wait_ge(piece_used, n0 + k + 1)
                        act.activation(xm_in[:, 2 * k:2 * k + 2, :], io(n0 + k), ACT.Copy).then_inc(proj_ready, 1)
                        if k:
                            conv_silu(k - 1)
                    elif step == "z":
                        hi_ahead(n0 + k + 10)
                        act.wait_ge(piece_used, n0 + k + 9)
                        act.activation(ZS[:, 2 * k:2 * k + 2, :], io(n0 + 8 + k), ACT.Silu).then_inc(proj_ready, 1)
                        if k == 0:
                            conv_silu(7)
                            act.wait_ge(m_bd_used, 16)
                            for q in range(4):
                                ins = act.activation(GE[:, 8 * q:8 * q + 8, :],
                                                     PS[q][:, 0:288].rearrange("p (t g) -> p t g", t=8), ACT.Copy)
                            ins.then_inc(m_gsb, 1)
                    elif step == "gates":
                        act.wait_ge(m_gates, 1)
                        act.activation(f_row, MISC[32:32 + MH, 0:T], ACT.Copy)
                        act.activation(i_row, MISC[0:MH, 0:T], ACT.Copy).then_inc(m_rows, 1)
                        act.wait_ge(m_rowd, 1)
                        link(act.activation(ln_row, f_row, ACT.Abs))
                        chained()
                        link(act.activation(ln_row, ln_row, ACT.Exp, scale=-1.0))
                        chained()
                        act.activation(ln_row, ln_row, ACT.Ln, bias=ones[0:MH, 0:1]).then_inc(m_rows, 1)
                        act.wait_ge(m_rowd, 2)
                        act.activation(em_row, f_row, ACT.Exp, scale=-1.0).then_inc(m_rows, 1)
                    elif step == "cols":
                        act.wait_ge(m_colT, 1)
                        act.activation(c_col, PS[2][:, 0:8], ACT.Copy).then_inc(m_rows, 1)
                    elif step == "a":
                        if k:
                            act.wait_ge(m_s, k)
                        for t in range(4):
                            act.wait_ge(m_qk, 4 * k + t + 1)
                            act.activation(QK[:, t, :], PS[0][:, :], ACT.Copy).then_inc(m_qks, 1)
                            if t % 2:
                                if k:
                                    act.wait_ge(m_num, k)
                                act.wait_ge(m_bd_used, 16 + 4 * k + t + 1)
                                dst = VH[:, :, 128 * (t - 1):128 * (t + 1)].rearrange("p b (t c) -> p t b c", t=2)
                                src = PS[2][:, :].rearrange("p (t b c) -> p t b c", t=2, b=TB)
                                for x in range(2):
                                    ins = act.activation(dst[:, x, :, :], src[:, x, :, :], ACT.Copy)
                                ins.then_inc(m_vs, 1)
                    elif step == "b":
                        act.wait_ge(m_e, k + 1)
                        act.activation(EW, EW, ACT.Exp, scale=-1.0).then_inc(m_ex, 1)
                    elif step == "d":
                        for x, buf in enumerate((gate_f, hid_f)):
                            act.wait_ge(m_hc, 2 * k + x + 1)
                            act.activation(buf.rearrange("p (t n) -> p t n", t=2),
                                           xm_in[:, 4 * k + 2 * x:4 * k + 2 * x + 2, :], ACT.Square).then_inc(m_sq, 1)
                    elif step == "e":
                        act.wait_ge(m_var, k + 1)
                        link(act.activation(lnb[:, :], PS[2][:, 0:T], ACT.Ln, bias=eps_c[:, 0:1], scale=1.0 / 512))
                        chained()
                        act.activation(rstd[:, :], lnb[:, :], ACT.Exp, scale=-0.5).then_inc(m_rs, 1)
                for k in range(16, 24):
                    hi_ahead(n0 + k + 2)
                finish_update(st)

            act.wait_ge(cols_ready, ROW_TILES)
            cc = cols[:, COL["c"]:COL["c"] + KT]
            act.activation(c_act[:, :], cc, ACT.Silu).then_inc(c_ready, 1)
            act.wait_ge(const_ready, 3)
            for k, t in enumerate((sin_t, cos_t)):
                act.wait_ge(rope_chain, ROPE_STEPS)
                act.activation(t[:, :], rope_w[2 + 2 * k], ACT.Sin).then_inc(rope_ready, 1)
            act.activation(lam_s[:, 0:4], lam_s[:, 0:4], ACT.Exp).then_inc(lam_ready, 1)
            if plan.subs:
                for q in range(4):
                    act.wait_ge(first_used, 2 * q + 2)
                    act.activation(first_row[:, 512 * q:512 * q + 512], PS[q][0:1, :], ACT.Copy).then_inc(first_copied, 1)
            for st in plan.steps:
                kind, idx = st["key"]
                if kind == "ffn":
                    ffn(st)
                elif kind in "ABC":
                    attention(st)
                elif kind == "mlstm":
                    mlstm(st)
                elif kind == "hyb":
                    hybrid(st)
                if st["key"] == ("ffn", 3):
                    final_norm(st)
            for q in range(4):
                act.wait_ge(outT, q + 1)
                act.activation(out_sb[:, q // 2, (q % 2) * 512:(q % 2 + 1) * 512], PS[4 + q][:, :],
                               ACT.Copy).then_inc(out_ready, 1)

        @block.vector
        def _(dve):
            nchain = [0]

            def link(ins):
                nchain[0] += 1
                ins.then_inc(dve_chain, 1)
                return nchain[0]

            def chained(n=None):
                dve.wait_ge(dve_chain, n or nchain[0])

            def lo_ahead(n0, i=None):
                if n0 >= NP:
                    return
                n = n0 if i is None else i * RING + n0
                s = n0 % RING
                dve.wait_ge(hi_ready, n + 1)
                dve.tensor_tensor(w_lo[:, s, :], w_raw[:, s, :], w_hi[:, s, :].bitcast(F32),
                                  ALU.subtract).then_inc(lo_ready, 1)

            def normalise(st):
                dve.wait_ge(rstd_ready, st["sq"] + 1)
                m = st["norm"]

                def lo(kt):
                    dve.wait_ge(hhi_ready, 8 * m + kt + 1)
                    if st["second"]:
                        ins = dve.tensor_tensor(h_lo[:, kt, :], work[:, kt, :], h_hi[:, kt, :].bitcast(F32),
                                                ALU.subtract)
                    else:
                        ins = dve.scalar_tensor_tensor(out=h_lo[:, kt, :], in0=work[:, kt, :],
                                                       scalar=mods[:, SUB[st["key"]], kt:kt + 1],
                                                       in1=h_hi[:, kt, :].bitcast(F32),
                                                       op0=ALU.add, op1=ALU.subtract)
                    ins.then_inc(hlo_ready, 1)

                for kt in range(KT):
                    scale = (col("norm_gains_2", NGAIN[st["key"]] * KT + kt) if st["second"]
                             else mods[:, SUB[st["key"]], KT + kt:KT + kt + 1])
                    dve.scalar_tensor_tensor(out=work[:, kt, :], in0=XT[:, kt, :], scalar=scale, in1=rstd[:, :],
                                             op0=ALU.mult, op1=ALU.mult).then_inc(t_ready, 1)
                    if kt >= 1:
                        lo(kt - 1)
                lo(KT - 1)

            def scaled_add(scale, source, last=None):
                marks = []

                def add(kt):
                    chained(marks[kt])
                    dve.tensor_tensor(XT[:, kt, :], XT[:, kt, :], work[:, kt, :], ALU.add).then_inc(xt_ready, 1)

                for kt in range(KT):
                    marks.append(link(dve.scalar_tensor_tensor(
                        out=work[:, kt, :], in0=source(kt), scalar=scale(kt), in1=rstd[:, :],
                        op0=ALU.mult, op1=ALU.mult)))
                    if kt:
                        add(kt - 1)
                add(KT - 1)

            def finish_update(st):
                if st["second"]:
                    dve.wait_ge(rstd_ready, st["sq"] + 2)
                    scaled_add(lambda kt: col("norm_gains_2", (NGAIN[st["key"]] + 1) * KT + kt), acc)
                    return
                if plan.subs and st is plan.steps[0]:
                    first_gate()
                k = plan.subs.index(SUB[st["key"]]) + 1
                if k < len(plan.subs):
                    modulation(k)
                for kt in range(KT):
                    bank_summed(dve, st, kt // 2)
                    dve.scalar_tensor_tensor(out=XT[:, kt, :], in0=acc(kt),
                                             scalar=mods[:, SUB[st["key"]], 2 * KT + kt:2 * KT + kt + 1],
                                             in1=XT[:, kt, :], op0=ALU.mult, op1=ALU.add).then_inc(xt_ready, 1)

            def final_norm(st):
                dve.wait_ge(rstd_ready, st["sq"] + 2)
                for kt in range(KT):
                    dve.scalar_tensor_tensor(out=XT[:, kt, :], in0=XT[:, kt, :], scalar=col("final_norm_g", kt),
                                             in1=rstd[:, :], op0=ALU.mult, op1=ALU.mult).then_inc(xt_ready, 1)

            def gate_piece(k):
                dve.wait_ge(gate_loaded, 32)
                w = first_w[:, 3 + k, :].rearrange("p (k n) -> p k n", k=KT)
                link(dve.tensor_tensor(w, w, c_act[:, :].unsqueeze(2).broadcast_to([P, KT, 256]), ALU.mult))
                chained()
                link(dve.tensor_tensor(w[:, 0:4, :], w[:, 0:4, :], w[:, 4:8, :], ALU.add))
                chained()
                link(dve.tensor_tensor(w[:, 0:2, :], w[:, 0:2, :], w[:, 2:4, :], ALU.add))
                chained()
                dve.tensor_tensor(gate_acc[:, 256 * k:256 * k + 256], w[:, 0, :], w[:, 1, :],
                                  ALU.add).then_inc(gate_dve, 1)

            def gate_column(s):
                half = 1.0 if s % 3 == 1 else 0.5
                link(dve.tensor_scalar(mods[:, s, 16:24], mods[:, s, 16:24], 1.0, half, ALU.add, ALU.mult))
                chained()

            def first_gate():
                s = plan.subs[0]
                dve.wait_ge(gate_sum, 1)
                c = COL["ada_b"] + 24 * s + 16
                if len(plan.subs) > 1:
                    dve.wait_ge(mod_sum, 1)
                link(dve.tensor_tensor(mods[:, s, 16:24], MISC[:, 280:288], cols[:, c:c + 8], ALU.add))
                chained()
                gate_column(s)

            def modulation(k):
                s = plan.subs[k]
                m = mods[:, s, :]
                n = 24 if k else 16
                if k:
                    dve.wait_ge(mod_sum, k)
                else:
                    dve.wait_ge(first_cols, 1)
                sums = MISC[:, 256:280] if k else PS[0][:, 0:16]
                link(dve.tensor_tensor(m[:, 0:n], sums, cols[:, COL["ada_b"] + 24 * s:COL["ada_b"] + 24 * s + n], ALU.add))
                chained()
                g = cols[:, COL["norm_g"] + 8 * s:COL["norm_g"] + 8 * s + 8]
                dve.scalar_tensor_tensor(out=m[:, 8:16], in0=m[:, 8:16], scalar=1.0, in1=g,
                                         op0=ALU.add, op1=ALU.mult).then_inc(mod_ready, 1)
                if k:
                    gate_column(s)
                dve.wait_ge(mod_ready, k + 1)

            def ffn(st):
                n, c0, d0 = st["piece"], CHUNKS * st["ffn"], st["down"]
                normalise(st)
                lo_ahead(n + 2)
                if plan.subs and st is plan.steps[0]:
                    gate_piece(0)
                lo_ahead(n + 3)
                if plan.subs and st is plan.steps[0]:
                    gate_piece(1)

                def gated(c, up_bank, u):
                    if not (type(c) is int and c == 0):
                        dve.wait_ge(hid_ready, c)
                    dve.wait_ge(silu_ready, c + 1)
                    dve.wait_ge(piece_used, u + 1)
                    dve.tensor_tensor(hid[:, :, :], gate_s[:, :, :], io(up_bank), ALU.mult).then_inc(hid_full, 1)

                def parts(c, freed):
                    dve.wait_ge(hid_full, c + 1)
                    if not (type(freed) is int and freed == 0):
                        dve.wait_ge(piece_used, freed)
                    mark = c * 1 + (chain0 + 1 - c0)
                    dve.tensor_copy(d_hi[:, 0, :, :], hid[:, :, :]).then_inc(dve_chain, 1)
                    dve.wait_ge(dve_chain, mark)
                    dve.tensor_tensor(d_lo[:, 0, :, :], hid[:, :, :], d_hi[:, 0, :, :].bitcast(F32),
                                      ALU.subtract).then_inc(hid_ready, 1)

                chain0 = nchain[0]
                gated(c0, n + 1, n + 1)
                parts(c0, n)

                def body(n0, i, c):
                    g = n0 if i is None else i * RING + n0
                    lo_ahead(n0 + 2, i)
                    lo_ahead(n0 + 3, i)
                    gated(c, n0 + 1, g + 1)
                    lo_ahead(n0 + 4, i)
                    parts(c, g + 3)

                body(n + 2, None, c0 + 1)
                with dve.Fori(1, CHUNKS - 2) as i:
                    body(n + 2, i, i + (c0 + 1))
                body(n + 2 + RING * (CHUNKS - 2), None, c0 + CHUNKS - 1)
                nchain[0] += CHUNKS
                lo_ahead(n + 3 * CHUNKS - 1 + 2)
                finish_update(st)

            def split_pair(st, c, src, ahead=True):
                rows0 = st["piece"] + PIECES[st["key"][0]] - PARTS[st["key"][0]]
                if c >= 2:
                    dve.wait_ge(piece_used, rows0 + c - 1)
                mark = link(dve.tensor_copy(d_hi[:, c % 2, :, :], src))
                chained(mark)
                dve.tensor_tensor(d_lo[:, c % 2, :, :], src, d_hi[:, c % 2, :, :].bitcast(F32),
                                  ALU.subtract).then_inc(parts_ready, 1)
                if ahead:
                    lo_ahead(rows0 + c + 2)

            def parts_of(st, source, ready):
                for c in range(PARTS[st["key"][0]]):
                    ready(c)
                    split_pair(st, c, source(c))

            def rotate(st, k):
                kind = st["key"][0]
                piece, nt = (k, 2 if k else 1) if kind == "C" else (k + 4, 2)
                dve.wait_ge(proj_ready, st["evac"] + piece + 1)
                if st["rots"] + k:
                    dve.wait_ge(roped, st["rots"] + k)
                if st["rots"] + k == 0:
                    dve.wait_ge(rope_ready, 2)
                cosb = cos_t[:, :].unsqueeze(1).broadcast_to([P, nt, T])
                sinb = sin_t[:, :].unsqueeze(1).broadcast_to([P, nt, T])
                link(dve.tensor_tensor(rot_a[:, 0:nt, :], raw_qk[:, k % 2, 0:nt, :], cosb, ALU.mult))
                dve.wait_ge(turned, st["rots"] + k + 1)
                m = MISC[:, 0:nt * T].rearrange("p (t n) -> p t n", t=nt)
                link(dve.tensor_tensor(rot_b[:, 0:nt, :], m, sinb, ALU.mult))
                chained()
                if kind == "C":
                    dst = K[:, 0:1, :] if k == 0 else Q[:, 2 * k - 2:2 * k, :]
                else:
                    dst = (K if k % 2 else Q)[:, k // 2 * 2:k // 2 * 2 + 2, :]
                if kind == "C" and k == 0:
                    link(dve.tensor_tensor(dst, rot_a[:, 0:nt, :], rot_b[:, 0:nt, :], ALU.add))
                    chained()
                    for m in range(2):
                        for h in range(2):
                            ins = dve.tensor_copy(KD[64 * h:64 * h + 64, m, :], K[64 * m:64 * m + 64, 0, :])
                    ins.then_inc(roped, 1)
                else:
                    dve.tensor_tensor(dst, rot_a[:, 0:nt, :], rot_b[:, 0:nt, :], ALU.add).then_inc(roped, 1)

            def stick_unit(st, u):
                if 1 <= u < 9:
                    dve.wait_ge(r_ready, u)
                    dve.wait_ge(nb_ready, u)
                    w = nb[:, (u - 1) % 2, :, :]
                    for h in range(2):
                        ins = dve.tensor_tensor(w[:, h, :], w[:, h, :], PS[2 + h][:, 0:384], ALU.subtract)
                    ins.then_inc(arg_ready, 1)
                if u < 8:
                    dve.wait_ge(ln_ready, u + 1)
                    if u:
                        dve.wait_ge(r_ready, u)
                    for h in range(2):
                        ins = dve.scalar_tensor_tensor(out=sp[:, h, :], in0=PS[h][:, 0:384], scalar=0.0,
                                                       in1=lnv[:, h, :], op0=ALU.max, op1=ALU.add)
                    ins.then_inc(sp_ready, 1)
                    if u >= 2:
                        dve.wait_ge(o_ready, st["att"] + u - 1)
                    w = nb[:, u % 2, :, :]
                    for h in range(2):
                        ins = dve.scalar_tensor_tensor(out=w[:, h, :], in0=PS[h][:, 0:384], scalar=0.0,
                                                       in1=lnv[:, h, :], op0=ALU.min, op1=ALU.subtract)
                    ins.then_inc(nb_ready, 1)

                if 1 <= u < 9:
                    dve.wait_ge(e_ready, u)
                    w = nb[:, (u - 1) % 2, :, :]
                    dve.tensor_tensor(w, w, strict[:, :].unsqueeze(1).broadcast_to([P, 2, 384]),
                                      ALU.mult).then_inc(a_ready, 1)

            SEG = ((0, 256), (256, 384))

            def soft_unit(st, u):
                kind = st["key"][0]
                if u < 8:
                    stat = stat_of[u % 2]
                    mask = a_mask if kind == "A" else c_mask
                    dve.wait_ge(s_ready, st["att"] + u + 1)
                    if u:
                        dve.wait_ge(p_ready, st["soft"] + u)
                    if u >= 2:
                        dve.wait_ge(w_ready, st["soft"] + u - 1)
                    for h in range(2):
                        link(dve.tensor_tensor(sc[:, h, :], PS[h][:, 0:384], mask[:, :], ALU.add))
                    chained()
                    for k, (lo_c, hi_c) in enumerate(SEG):
                        link(dve.tensor_reduce(stat[:, 2 * k:2 * k + 2], sc[:, :, lo_c:hi_c], AX_X, ALU.max))
                    chained()
                    if kind == "C":
                        sk = sinks[:, 2 * u:2 * u + 2].unsqueeze(1).broadcast_to([P, 2, 2])
                        mx = stat[:, 0:4].rearrange("p (k h) -> p k h", k=2)
                        link(dve.tensor_tensor(mx, mx, sk, ALU.max))
                        chained()
                        link(dve.tensor_tensor(stat[:, 12:16].rearrange("p (k h) -> p k h", k=2), sk, mx, ALU.subtract))
                    dve.tensor_scalar(stat[:, 4:8], stat[:, 0:4], -1.0, None, ALU.mult).then_inc(negm_ready, 1)
                if 1 <= u < 9:
                    pr, stat = pr_of[(u - 1) % 2], stat_of[(u - 1) % 2]
                    dve.wait_ge(p_ready, st["soft"] + u)
                    if u >= 2:
                        dve.wait_ge(wT_ready, st["soft"] + u - 1)
                    if kind == "C":
                        link(dve.tensor_tensor(stat[:, 8:12], stat[:, 8:12], stat[:, 12:16], ALU.add))
                        chained()
                    link(dve.reciprocal(stat[:, 8:12], stat[:, 8:12]))
                    chained()
                    if kind == "C":
                        for k, (lo_c, hi_c) in enumerate(SEG):
                            for h in range(2):
                                ins = dve.tensor_scalar(wts[:, h, lo_c:hi_c], pr[:, h, lo_c:hi_c],
                                                        stat[:, 8 + 2 * k + h:9 + 2 * k + h], None, ALU.mult)
                    else:
                        i = st["key"][1]
                        for k in range(2):
                            c = 9 + 2 * k
                            link(dve.tensor_tensor(stat[:, c:c + 1], stat[:, c:c + 1], lam[:, i:i + 1], ALU.mult))
                        chained()
                        for k, (lo_c, hi_c) in enumerate(SEG):
                            link(dve.tensor_scalar(wts[:, 1, lo_c:hi_c], pr[:, 1, lo_c:hi_c],
                                                   stat[:, 9 + 2 * k:10 + 2 * k], None, ALU.mult))
                        chained()
                        for k, (lo_c, hi_c) in enumerate(SEG):
                            ins = dve.scalar_tensor_tensor(out=wts[:, 0, lo_c:hi_c], in0=pr[:, 0, lo_c:hi_c],
                                                           scalar=stat[:, 8 + 2 * k:9 + 2 * k],
                                                           in1=wts[:, 1, lo_c:hi_c], op0=ALU.mult, op1=ALU.add)
                    ins.then_inc(w_ready, 1)

            def attention(st):
                kind, n0 = st["key"][0], st["piece"]
                normalise(st)
                for step, k in sequence(kind):
                    if step == "in":
                        lo_ahead(n0 + k + 2)
                    elif step == "rot":
                        rotate(st, k)
                    else:
                        (stick_unit if kind == "B" else soft_unit)(st, k)
                def ready(c):
                    dve.wait_ge(ot_ready, st["att"] + 2 * c + 2)
                    if kind == "A":
                        i = st["key"][1]
                        dve.wait_ge(sub_rstd, st["soft_a"] + c + 1)
                        v = OT[:, 2 * c:2 * c + 2, :]
                        link(dve.scalar_tensor_tensor(out=v, in0=v, scalar=sub_g[:, i:i + 1],
                                                      in1=osl[:, 2 * c:2 * c + 2, :], op0=ALU.mult, op1=ALU.mult))
                        chained()

                parts_of(st, lambda c: OT[:, 2 * c:2 * c + 2, :], ready)
                finish_update(st)

            def convolve(src, dst, tiles, name, ready, done, bias=None):
                ready()
                marks = {}
                n_tiles = SIZES[name] // 4
                for w in range(4):
                    for t in tiles:
                        if w:
                            chained(marks[t])
                        x, o, c = src(t)[:, w:w + T], dst(t), col(name, w * n_tiles + t)
                        if w == 0:
                            if bias is None:
                                ins = dve.tensor_scalar(o, x, c, None, ALU.mult)
                            else:
                                ins = dve.tensor_scalar(o, x, c, col(bias, t), ALU.mult, ALU.add)
                        else:
                            ins = dve.scalar_tensor_tensor(out=o, in0=x, scalar=c, in1=o, op0=ALU.mult, op1=ALU.add)
                        if w == 3 and t == tiles[-1]:
                            ins.then_inc(done, 1)
                        else:
                            marks[t] = link(ins)

            def hybrid(st):
                n0 = st["piece"]
                normalise(st)
                link(dve.memset(XR[:, :, 0:3], 0.0))
                link(dve.memset(BCR[:, :, 0:3], 0.0))
                biases = cols[:, COL["lru_ba"]:COL["lru_ba"] + 16]
                link(dve.tensor_scalar(biases, biases, 0.5, None, ALU.mult))
                link(dve.tensor_scalar(lam_4, cols[:, COL["lru_lambda"]:COL["lru_lambda"] + 8], -1.0, 0.0,
                                       ALU.mult, ALU.max))
                chained()
                dve.wait_ge(y_lam_ln, 1)
                link(dve.tensor_tensor(sp_lam, sp_lam, lam_4, ALU.add))
                chained()
                link(dve.tensor_scalar(lam_4, sp_lam, -2.0, None, ALU.mult))
                dve.tensor_scalar(lam_2, sp_lam, -4.0, None, ALU.mult).then_inc(y_lam, 1)
                for step, k in hybrid_sequence():
                    if step == "in":
                        lo_ahead(n0 + k + 2)

                        def ready():
                            dve.wait_ge(proj_ready, st["evac"] + k + 1)
                            if k in (0, 8):
                                chained()
                        if k < 4:
                            convolve(lambda t: XR[:, t, :], lambda t: XL[:, t, :], (2 * k, 2 * k + 1),
                                     "lru_conv_w", ready, y_conv, "lru_conv_b")
                        elif k in (8, 9):
                            convolve(lambda t: BCR[:, t - 8, :], lambda t: BC[:, t - 8, :], (2 * k - 8, 2 * k - 7),
                                     "ssd_conv_w", ready, y_bc_conv)
                        elif 10 <= k < 14:
                            convolve(lambda t: XR[:, t, :], lambda t: XS[:, t, :], (2 * k - 20, 2 * k - 19),
                                     "ssd_conv_w", ready, y_xs_conv)
                    elif step == "row":
                        c = k + 1
                        if 2 <= c < 4:
                            split_pair(st, c, GL[:, 2 * c:2 * c + 2, :], False)
                        elif 4 <= c < 8:
                            dve.wait_ge(y_ssd, c - 3)
                            split_pair(st, c, ZG[:, 2 * c - 8:2 * c - 6, :], False)
                        lo_ahead(n0 + 18 + k + 2)
                    elif step == "mix":
                        dve.wait_ge(y_th, 8)
                        dve.wait_ge(y_conv, 4)
                        link(dve.scalar_tensor_tensor(out=TI, in0=TI, scalar=1.0, in1=XL, op0=ALU.add, op1=ALU.mult))
                        chained()
                        dve.wait_ge(y_decay, 1)
                        link(dve.scalar_tensor_tensor(out=TI, in0=work[:, :, :], scalar=1.0, in1=TI, op0=ALU.add,
                                                      op1=ALU.mult))
                        chained()
                        dve.scalar_tensor_tensor(out=TI, in0=RC, scalar=0.5, in1=TI, op0=ALU.mult,
                                                 op1=ALU.mult).then_inc(y_mix, 1)
                    elif step == "scan":
                        dve.wait_ge(y_mix, 1)
                        for t in range(KT):
                            link(dve.tensor_tensor_scan(XL[:, t, :], work[:, t, :], TI[:, t, :], 0.0,
                                                        ALU.mult, ALU.add))
                    elif step == "y_lru":
                        chained()
                        dve.tensor_tensor(GL, XL, GL, ALU.mult).then_inc(y_scan, 1)
                    elif step == "cb":
                        dve.wait_ge(y_cb, 1)
                        for g in range(2):
                            ins = dve.tensor_tensor(CB[:, g, :], PS[g][:, 0:384], causal[:, :], ALU.mult)
                        ins.then_inc(y_cb_read, 1)
                    elif step == "xs_t":
                        dve.wait_ge(y_dta, 1)
                        dve.wait_ge(y_scan, 1)
                        for q in range(4):
                            dve.wait_ge(y_xst, q + 1)
                            b, half = q // 2, q % 2
                            dve.tensor_tensor(XC_T[:, b, half * 512:half * 512 + 512].rearrange("p (h c) -> p h c", h=8),
                                              PS[q][:, :].rearrange("p (h c) -> p h c", h=8),
                                              dt[:, b, 8 * half:8 * half + 8].unsqueeze(2).broadcast_to([P, 8, 64]),
                                              ALU.mult).then_inc(y_xc, 1)
                        for c in range(2):
                            split_pair(st, c, GL[:, 2 * c:2 * c + 2, :], False)
                    elif step == "dt":
                        if k == 0:
                            dve.wait_ge(y_loaded, 32)
                            dve.wait_ge(y_dt, 1)
                            bias = dt_bias.unsqueeze(1).broadcast_to([P, TB, 16])
                            dve.tensor_tensor(dt, MISC[:, 0:32].rearrange("p (b h) -> p b h", b=TB), bias,
                                              ALU.add).then_inc(y_dt_raw, 1)
                        elif k == 1:
                            dve.wait_ge(y_dt_raw, 1)
                            dve.wait_ge(y_dt_ln, 1)
                            link(dve.scalar_tensor_tensor(out=dt, in0=dt, scalar=0.0, in1=dt_ln, op0=ALU.max, op1=ALU.add))
                            chained()
                            av = a_log.unsqueeze(1).broadcast_to([P, TB, 16])
                            dve.scalar_tensor_tensor(out=dta, in0=dt, scalar=-1.0, in1=av, op0=ALU.mult,
                                                     op1=ALU.mult).then_inc(y_dta, 1)
                    elif step == "decay":
                        if k == 0:
                            dve.wait_ge(y_acs, 2)
                            dve.wait_ge(y_gates, 8)
                            dve.wait_ge(y_cb_read, 1)
                        if k >= 2:
                            dve.wait_ge(y_o, k - 1)
                        dve.wait_ge(y_r, k + 1)
                        e, r = decay_of(k), PS[4 + k % 2]
                        for x in range(2):
                            h = 2 * k + x
                            dve.tensor_scalar(e[:, x, 0:T], r[:, x * T:x * T + T], acs_c[:, 0, h:h + 1], 0.0,
                                              ALU.subtract, ALU.min)
                            ins = dve.tensor_scalar(e[:, x, T:384], r[:, x * T + P:x * T + T], acs_c[:, 1, h:h + 1], 0.0,
                                                    ALU.subtract, ALU.min)
                        ins.then_inc(y_e, 1)
                        dve.wait_ge(y_ex, k + 1)
                        g = k // 4
                        dve.tensor_tensor(e, e, CB[:, g, :].unsqueeze(1).broadcast_to([P, 2, 384]),
                                          ALU.mult).then_inc(y_w, 1)
                    elif step == "head":
                        dve.wait_ge(y_o, k + 1)
                        dve.wait_ge(proj_ready, st["evac"] + 18)
                        for x in range(2):
                            rows = slice(64 * x, 64 * x + 64)
                            link(dve.scalar_tensor_tensor(out=XS[rows, k, :], in0=XS[rows, k, :], scalar=d_col[rows, k:k + 1],
                                                          in1=PS[6 + k % 2][rows, x * T:x * T + T],
                                                          op0=ALU.mult, op1=ALU.add))
                        chained()
                        dve.tensor_tensor(ZG[:, k, :], ZG[:, k, :], XS[:, k, :], ALU.mult).then_inc(y_y, 1)
                    elif step == "norm":
                        dve.wait_ge(y_rs, 1)
                        dve.wait_ge(y_y, 8)
                        for t in range(KT):
                            ins = dve.scalar_tensor_tensor(out=ZG[:, t, :], in0=ZG[:, t, :], scalar=col("ssd_norm_g", t),
                                                           in1=hyb_rs[:, t // 4, :], op0=ALU.mult, op1=ALU.mult)
                            if t % 2:
                                ins.then_inc(y_ssd, 1)
                finish_update(st)

            def mlstm(st):
                n0 = st["piece"]
                normalise(st)
                link(dve.memset(XM[:, :, 0:3], 0.0))
                builds = [0]

                def block_diagonal(kinds, t):
                    n = builds[0]
                    builds[0] += 1
                    if n >= 2:
                        dve.wait_ge(m_bd_used, n - 1)
                    dve.tensor_tensor(BD[:, n % 2, :, :].rearrange("p k (n o) -> p k n o", n=32),
                                      blocks[:, :].unsqueeze(1).unsqueeze(3).broadcast_to([P, 3, 32, 4]),
                                      w4[:, kinds:kinds + 3, t, :].unsqueeze(2).broadcast_to([P, 3, 32, 4]),
                                      ALU.mult).then_inc(m_bd, 1)

                for step, k in mlstm_sequence():
                    if step == "xm":
                        lo_ahead(n0 + k + 2)
                        if k == 0:
                            dve.wait_ge(m_loaded, 48)
                        block_diagonal(3, 2 * k)
                        block_diagonal(3, 2 * k + 1)

                        def ready():
                            dve.wait_ge(proj_ready, st["evac"] + k + 1)
                            if k == 0:
                                chained()
                        convolve(lambda t: XM[:, t, :], lambda t: XC[:, t, :], (2 * k, 2 * k + 1),
                                 "mlstm_conv_w", ready, m_conv)
                    elif step == "z":
                        lo_ahead(n0 + k + 10)
                    elif step == "gates":
                        dve.wait_ge(m_rows, 1)
                        link(dve.tensor_scalar(f_row, f_row, b_gate[0:MH, 1:2], None, ALU.add))
                        dve.tensor_scalar(i_row, i_row, b_gate[0:MH, 0:1], None, ALU.add).then_inc(m_rowd, 1)
                        dve.wait_ge(m_rows, 2)
                        dve.wait_ge(m_rowd, 1)
                        link(dve.scalar_tensor_tensor(out=f_row, in0=f_row, scalar=0.0, in1=ln_row,
                                                      op0=ALU.min, op1=ALU.subtract))
                        chained()
                        link(dve.tensor_tensor_scan(b_row, ones[0:MH, 0:1].broadcast_to([MH, T]), f_row, 0.0,
                                                    ALU.mult, ALU.add))
                        chained()
                        link(dve.tensor_tensor(i_row, i_row, b_row, ALU.subtract))
                        chained()
                        link(dve.tensor_tensor_scan(m_row, i_row, i_row, 0.0, ALU.max, ALU.max))
                        chained()
                        dve.tensor_tensor(f_row, b_row, m_row, ALU.add).then_inc(m_rowd, 1)
                    elif step == "a":
                        for t in range(4):
                            block_diagonal(0, 4 * k + t)
                    elif step == "b":
                        dve.wait_ge(m_mb, k + 1)
                        if k == 0:
                            dve.wait_ge(m_rows, 4)
                        else:
                            dve.wait_ge(m_var, k)
                        dve.tensor_scalar(EW[:, 0:T], PS[1][:, 0:T], c_col[:, k:k + 1], 0.0, ALU.subtract, ALU.max)
                        dve.tensor_scalar(EW[:, T:384], PS[1][:, P:T], c_col[:, MH + k:MH + k + 1], 0.0,
                                          ALU.subtract, ALU.max).then_inc(m_e, 1)
                        dve.wait_ge(m_ex, k + 1)
                        link(dve.tensor_tensor(EW, EW, causal[:, :], ALU.mult))
                        chained()
                        dve.wait_ge(m_s, k + 1)
                        dve.scalar_tensor_tensor(out=WW, in0=PS[0][:, 0:384], scalar=float(512 ** -0.5), in1=EW,
                                                 op0=ALU.mult, op1=ALU.mult).then_inc(m_w, 1)
                    elif step == "c":
                        dve.wait_ge(m_den, k + 1)
                        if k:
                            dve.wait_ge(m_rs, k)
                            dve.wait_ge(m_hh, k)
                        link(dve.tensor_copy(lnb[:, :], PS[1][:, T:2 * T]))
                        chained()
                        link(dve.tensor_tensor(lnb[:, :], PS[2][:, 0:T], lnb[:, :], ALU.max))
                        chained()
                        dve.scalar_tensor_tensor(out=lnb[:, :], in0=PS[2][:, 0:T], scalar=-1.0, in1=lnb[:, :],
                                                 op0=ALU.mult, op1=ALU.max).then_inc(m_absd, 1)
                        dve.wait_ge(m_absd, k + 1)
                        link(dve.reciprocal(lnb[:, :], lnb[:, :]))
                        chained()
                        dve.wait_ge(m_num, k + 1)
                        rb = lnb[:, :].unsqueeze(1).broadcast_to([P, 2, T])
                        for x, bank in enumerate((PS[3], MISC)):
                            ins = dve.tensor_tensor(xm_in[:, 4 * k + 2 * x:4 * k + 2 * x + 2, :],
                                                    bank[:, :].rearrange("p (t n) -> p t n", t=2), rb, ALU.mult)
                        ins.then_inc(m_hh, 1)
                    elif step == "d":
                        dve.wait_ge(m_mean, k + 1)
                        dve.wait_ge(m_hh, k + 1)
                        for t in range(4):
                            h = xm_in[:, 4 * k + t, :]
                            ins = dve.scalar_tensor_tensor(out=h, in0=PS[2][:, 0:T], scalar=-1.0 / 512, in1=h,
                                                           op0=ALU.mult, op1=ALU.add)
                            if t % 2:
                                ins.then_inc(m_hc, 1)
                    elif step == "e":
                        dve.wait_ge(m_rs, k + 1)
                        dve.wait_ge(m_hc, 2 * k + 2)
                        marks = []
                        for t in range(4 * k, 4 * k + 4):
                            h = xm_in[:, t, :]
                            marks.append(link(dve.scalar_tensor_tensor(
                                out=h, in0=h, scalar=col("mlstm_norm_g", t), in1=rstd[:, :],
                                op0=ALU.mult, op1=ALU.mult)))
                        for i, t in enumerate(range(4 * k, 4 * k + 4)):
                            h = xm_in[:, t, :]
                            chained(marks[i])
                            marks[i] = link(dve.scalar_tensor_tensor(
                                out=h, in0=XC[:, t, :], scalar=col("mlstm_skip", t), in1=h,
                                op0=ALU.mult, op1=ALU.add))
                        dve.wait_ge(proj_ready, st["evac"] + min(16, 8 + 2 * k + 2))
                        for i, t in enumerate(range(4 * k, 4 * k + 4)):
                            h = xm_in[:, t, :]
                            chained(marks[i])
                            ins = dve.tensor_tensor(h, h, ZS[:, t, :], ALU.mult)
                            if t % 4 < 3:
                                link(ins)
                        ins.then_inc(m_y, 1)
                        if k == MH - 2:
                            dve.wait_ge(m_y, 1)
                            for c in range(2):
                                split_pair(st, c, xm_in[:, 2 * c:2 * c + 2, :], False)
                for c in range(PARTS["mlstm"]):
                    if c >= 2:
                        dve.wait_ge(m_y, c // 2 + 1)
                        split_pair(st, c, xm_in[:, 2 * c:2 * c + 2, :], False)
                    lo_ahead(n0 + 16 + c + 2)
                finish_update(st)

            def rotary_tables():
                steps = [0]

                def step(ins):
                    steps[0] += 1
                    ins.then_inc(rope_chain, 1)
                    dve.wait_ge(rope_chain, steps[0])

                dve.wait_ge(small_loaded, 64)
                ang = rope_w[0]
                step(dve.tensor_copy(rope_w[1], pos_i[:, :]))
                step(dve.tensor_scalar(ang, rope_w[1], inv_freq[:, 0:1], None, ALU.mult))
                for k, off in enumerate((0.0, float(np.pi / 2))):
                    x, turns = rope_w[2 + 2 * k], rope_w[3 + 2 * k]
                    step(dve.tensor_scalar(turns, ang, float(1 / (2 * np.pi)), off / (2 * float(np.pi)), ALU.mult, ALU.add))
                    step(dve.tensor_scalar(turns, turns, MAGIC, None, ALU.add))
                    step(dve.tensor_scalar(turns, turns, -MAGIC, None, ALU.add))
                    step(dve.scalar_tensor_tensor(out=x, in0=turns, scalar=-TURN[0], in1=ang, op0=ALU.mult, op1=ALU.add))
                    step(dve.scalar_tensor_tensor(out=x, in0=turns, scalar=-TURN[1], in1=x, op0=ALU.mult, op1=ALU.add))
                    step(dve.scalar_tensor_tensor(out=x, in0=turns, scalar=-TURN[2], in1=x, op0=ALU.mult, op1=ALU.add))
                    step(dve.tensor_scalar(x, x, off, 3.1415925, ALU.add, ALU.min))
                    step(dve.tensor_scalar(x, x, -3.1415925, None, ALU.max))
                pairs = lam_w.rearrange("p i (k t) c -> p i k t c", t=2)
                for i in range(2):
                    step(dve.tensor_tensor(lam_p[:, i, :, :], pairs[:, i, :, 0, :], pairs[:, i, :, 1, :], ALU.mult))
                step(dve.tensor_reduce(lam_s[:, 0:4], lam_p.rearrange("p i k c -> p (i k) c"), AX_X, ALU.add))
                assert steps[0] == ROPE_STEPS
                dve.wait_ge(lam_ready, 1)
                for i in range(2):
                    link(dve.tensor_tensor(lam[:, i:i + 1], lam_s[:, 2 * i + 1:2 * i + 2], lam_s[:, 2 * i:2 * i + 1],
                                           ALU.subtract))
                    chained()
                    link(dve.tensor_scalar(lam[:, i:i + 1], lam[:, i:i + 1], -LAM_INIT[i], None, ALU.add))
                    link(dve.tensor_scalar(sub_g[:, i:i + 1], col("a_subln_2", i), 1.0 - LAM_INIT[i], None, ALU.mult))
                chained()

            for r in range(ROW_TILES):
                dve.wait_ge(rowsT, r + 1)
                dve.tensor_copy(cols[:, r * P:(r + 1) * P], PS[r % 4][:, 0:P]).then_inc(cols_ready, 1)
            dve.wait_ge(cols_ready, ROW_TILES)
            rotary_tables()
            for j in range(4):
                dve.wait_ge(xin_T, j + 1)
                for t in range(2):
                    dve.tensor_copy(XT[:, 2 * j + t, :], PS[4 + j][:, t * T:t * T + T]).then_inc(xt_ready, 1)
            for n in range(2):
                lo_ahead(n)
            dve.wait_ge(masks_ready, 1)
            if plan.subs:
                modulation(0)
            for st in plan.steps:
                kind, idx = st["key"]
                if kind == "ffn":
                    ffn(st)
                elif kind in "ABC":
                    attention(st)
                elif kind == "mlstm":
                    mlstm(st)
                elif kind == "hyb":
                    hybrid(st)
                if st["key"] == ("ffn", 3):
                    final_norm(st)

        @block.tensor
        def _(pe):
            def exact(o, whi, wlo, xhi, xlo, start, stop):
                pe.matmul(o, whi, xhi, start=start, stop=False, skip_group_check=True)
                pe.matmul(o, whi, xlo, start=False, stop=False, skip_group_check=True)
                return pe.matmul(o, wlo, xhi, start=False, stop=stop, skip_group_check=True)

            def split_ready(n0, i=None):
                n = n0 if i is None else i * RING + n0
                pe.wait_ge(lo_ready, n + 1)
                s = n0 % RING
                return w_hi[:, s, :], w_lo[:, s, :]

            def project(n0, i=None, norm=None):
                whi, wlo = split_ready(n0, i)
                order = [(t, kt) for t in range(2) for kt in range(KT)]
                if norm is not None:
                    order = [(t, kt) for kt in range(KT) for t in range(2)]
                for t, kt in order:
                    if norm is not None and t == 0:
                        pe.wait_ge(hlo_ready, 8 * norm + kt + 1)
                    c = kt * 256 + t * P
                    last = exact(io(n0)[:, t, :], whi[:, c:c + P], wlo[:, c:c + P], h_hi[:, kt, :], h_lo[:, kt, :],
                                 kt == 0 and (t == 0 or norm is None), kt == KT - 1)
                last.then_inc(piece_used, 1)

            def down(n0, i, buf, first, final):
                whi, wlo = split_ready(n0, i)
                for m in range(KT):
                    for j in range(2):
                        c = j * D + m * P
                        last = exact(acc(m), whi[:, c:c + P], wlo[:, c:c + P], d_hi[:, buf, j, :],
                                     d_lo[:, buf, j, :], first and j == 0 and m % 2 == 0, final and j == 1)
                    if final and m % 2 and m < KT - 1:
                        last.then_inc(acc_done, 1)
                last.then_inc(piece_used, 1)

            def sum_squares(e):
                for kt in range(KT):
                    if kt % 2 == 0:
                        pe.wait_ge(sq_ready, 4 * e + kt // 2 + 1)
                    last = pe.matmul(MISC[:, 0:T], ones[:, :], work[:, kt, :], start=(kt == 0), stop=(kt == KT - 1))
                last.then_inc(ss_ready, 1)

            def next_columns(st):
                if st["second"] or not plan.subs:
                    return
                pe.wait_ge(rstd_ready, st["sq"] + 1)
                if st is plan.steps[0]:
                    pe.wait_ge(gate_sub, 1)
                    pe.wait_ge(gate_dve, 2)
                    for j in range(8):
                        last = pe.matmul(MISC[:, 280 + j:281 + j], gate_acc[:, j * P:(j + 1) * P], ones[:, 0:1],
                                         start=True, stop=True)
                    last.then_inc(gate_sum, 1)
                k = plan.subs.index(SUB[st["key"]]) + 1
                if k < len(plan.subs):
                    pe.wait_ge(ada_sub, k)
                    for j in range(24):
                        last = pe.matmul(MISC[:, 256 + j:257 + j], ada_acc[:, j * P:(j + 1) * P], ones[:, 0:1],
                                         start=True, stop=True)
                    last.then_inc(mod_sum, 1)

            def finish_update(st):
                if st["second"]:
                    sum_squares(st["sq"] + 1)

            def values(n0, norm, c=0, width=256, out=None):
                whi, wlo = split_ready(n0)
                for b in range(TB):
                    for kt in range(KT):
                        if norm is not None and b == 0:
                            pe.wait_ge(hlo_ready, 8 * norm + kt + 1)
                        w = slice(kt * 256 + c, kt * 256 + c + width)
                        t = slice(b * P, (b + 1) * P)
                        o = io(n0)[:, b, :] if out is None else out(b)
                        last = exact(o, h_hi[:, kt, t], h_lo[:, kt, t], whi[:, w], wlo[:, w], kt == 0, kt == KT - 1)
                last.then_inc(piece_used, 1)

            def attention_input(st, i):
                kind, n = st["key"][0], st["piece"] + i
                norm = st["norm"] if i == 0 else None
                if i >= RING:
                    pe.wait_ge(proj_ready, st["evac"] + i - 2)
                if kind == "C" and i == 0:
                    whi, wlo = split_ready(n)
                    for kt in range(KT):
                        pe.wait_ge(hlo_ready, 8 * norm + kt + 1)
                        c = kt * 256
                        exact(io(n)[:, 0, :], whi[:, c:c + P], wlo[:, c:c + P], h_hi[:, kt, :], h_lo[:, kt, :],
                              kt == 0, kt == KT - 1)
                    values(n, None, P, P, lambda b: io(n)[:, 1, b * P:(b + 1) * P])
                elif kind != "C" and i < 4:
                    values(n, norm)
                else:
                    project(n)

            def turn_pair(st, k, units):
                kind = st["key"][0]
                piece, nt = (k, 2 if k else 1) if kind == "C" else (k + 4, 2)
                pe.wait_ge(proj_ready, st["evac"] + piece + 1)
                if st["rots"] + k:
                    pe.wait_ge(roped, st["rots"] + k)
                if st["att"] + units:
                    pe.wait_ge(ot_ready, st["att"] + units)
                m = MISC[:, 0:nt * T].rearrange("p (t n) -> p t n", t=nt)
                pe.matmul(m, turn[:, :], raw_qk[:, k % 2, 0:nt, :], start=True, stop=True).then_inc(turned, 1)

            def scores(st, u, rots):
                kind = st["key"][0]
                if kind == "B":
                    pe.wait_ge(proj_ready, st["evac"] + 6 + 2 * (u // 2))
                    if u:
                        pe.wait_ge(nb_ready, u)
                else:
                    pe.wait_ge(roped, st["rots"] + rots)
                    if st["soft"] + u:
                        pe.wait_ge(negm_ready, st["soft"] + u)
                for h in range(2):
                    rows = slice(64 * h, 64 * h + 64)
                    if kind == "B":
                        pe.matmul(PS[h][:, 0:256], K[rows, u, 0:P], Q[rows, u, :], start=True, stop=True)
                        last = pe.matmul(PS[h][:, 256:384], K[rows, u, P:T], Q[rows, u, P:T], start=True, stop=True)
                    else:
                        keys = K[rows, u, :] if kind == "A" else KD[rows, u // 4, :]
                        pe.matmul(PS[h][:, 0:256], Q[rows, u, P:T], keys, start=True, stop=True)
                        last = pe.matmul(PS[h][:, 256:384], Q[rows, u, 0:P], keys[:, 0:P], start=True, stop=True)
                last.then_inc(s_ready, 1)

            def later_sums(u):
                pe.wait_ge(spm_ready, u + 1)
                if u:
                    pe.wait_ge(arg_ready, u)
                for h in range(2):
                    o = PS[2 + h]
                    pe.matmul(o[:, 0:256], later[:, :], sp[:, h, 0:256], start=True, stop=False, skip_group_check=True)
                    pe.matmul(o[:, P:256], ones[:, :], sp[:, h, 256:384], start=False, stop=False, skip_group_check=True)
                    last = pe.matmul(o[:, 256:384], later[:, :], sp[:, h, 256:384], start=False, stop=True,
                                     skip_group_check=True)
                last.then_inc(r_ready, 1)

            def weigh(st, u, rots):
                kind = st["key"][0]
                if kind == "B":
                    pe.wait_ge(a_ready, u + 1)
                else:
                    pe.wait_ge(wTs_ready, st["soft"] + u + 1)
                if st["att"] + u:
                    pe.wait_ge(ot_ready, st["att"] + u)
                if st["rots"] + rots:
                    pe.wait_ge(roped, st["rots"] + rots)
                for h in range(1 if kind == "A" else 2):
                    w = nb[:, u % 2, h, :] if kind == "B" else wT[:, h, :]
                    v = [VD[:, b, u // 4, :] if kind == "C" else V[:, b, u * P:(u + 1) * P] for b in range(TB)]
                    pe.matmul(MISC[:, h * T:(h + 1) * T], v[0], w[:, 0:256], start=True, stop=False,
                              skip_group_check=True)
                    last = pe.matmul(MISC[:, h * T + P:(h + 1) * T], v[1], w[:, 256:384], start=False, stop=True,
                                     skip_group_check=True)
                last.then_inc(o_ready, 1)

            def transposed_weights(st, u):
                pe.wait_ge(w_ready, st["soft"] + u + 1)
                if st["soft"] + u:
                    pe.wait_ge(wTs_ready, st["soft"] + u)
                for h in range(1 if st["key"][0] == "A" else 2):
                    for src, dst in ((256, 0), (0, 128), (128, 256)):
                        last = pe.transpose(PS[2 + h][:, dst:dst + P], wts[:, h, src:src + P], ident[:, :])
                last.then_inc(wT_ready, 1)

            def down_part(st, c):
                n, parts = st["piece"] + PIECES[st["key"][0]], PARTS[st["key"][0]]
                if c == parts - 1:
                    if st["key"][0] == "mlstm":
                        pe.wait_ge(m_hh, MH)
                    next_columns(st)
                pe.wait_ge(parts_ready, st["parts"] + c + 1)
                down(n - parts + c, None, c % 2, c == 0, c == parts - 1)

            def down_all(st):
                for c in range(PARTS[st["key"][0]]):
                    down_part(st, c)

            def attention(st):
                kind = st["key"][0]
                sum_squares(st["sq"])
                units = rots = 0
                for step, k in sequence(kind):
                    if step == "in":
                        attention_input(st, k)
                    elif step == "rot":
                        turn_pair(st, k, units)
                        rots += 1
                    else:
                        if kind == "B":
                            if k >= 2:
                                weigh(st, k - 2, rots)
                            if k < 8:
                                scores(st, k, rots)
                            if 1 <= k < 9:
                                later_sums(k - 1)
                            continue
                        if k < 8:
                            scores(st, k, rots)
                        if 2 <= k < 10:
                            transposed_weights(st, k - 2)
                        if k >= 3:
                            weigh(st, k - 3, rots)
                            units = k - 2
                if kind == "A":
                    for j in range(4):
                        pe.wait_ge(sub_sq, st["soft_a"] + j + 1)
                        pe.matmul(accp(j), ones[:, :], osq[:, 2 * j:2 * j + 2, :].rearrange("p t n -> p (t n)"),
                                  start=True, stop=True).then_inc(sub_sum, 1)
                    pe.wait_ge(sub_ln, st["soft_a"] + 4)
                down_all(st)
                finish_update(st)

            def two_blocks(o, first, second, w, opened=True):
                pe.matmul(o[:, 0:T], first, w[:, 0:T], start=opened, stop=False, skip_group_check=True)
                return pe.matmul(o[:, P:T], second, w[:, T:384], start=False, stop=True, skip_group_check=True)

            def hybrid(st):
                n0 = st["piece"]
                sum_squares(st["sq"])
                for step, k in hybrid_sequence():
                    if step == "in":
                        if k >= RING:
                            pe.wait_ge(proj_ready, st["evac"] + k - 2)
                        project(n0 + k, norm=st["norm"] if k == 0 else None)
                    elif step == "row":
                        if k == 0:
                            pe.wait_ge(y_xc, 4)
                        down_part(st, k)
                    elif step == "lru":
                        if k == 0:
                            pe.wait_ge(y_loaded, 32)
                        pe.wait_ge(y_conv, k + 1)
                        for t in (2 * k, 2 * k + 1):
                            if t >= 4:
                                pe.wait_ge(y_th, t - 3)
                            for x in range(2):
                                last = pe.matmul(PS[t % 4][:, x * T:x * T + T], WAX[:, x, t, :], XL[:, t, :],
                                                 start=True, stop=True)
                            last.then_inc(y_gates, 1)
                    elif step == "cb":
                        pe.wait_ge(y_bc, 2)
                        pe.wait_ge(y_th, 8)
                        for g in range(2):
                            pe.matmul(PS[g][:, 0:T], BC[:, g, 0:P], BC[:, 2 + g, :], start=True, stop=True)
                            last = pe.matmul(PS[g][:, T:384], BC[:, g, P:T], BC[:, 2 + g, P:T], start=True, stop=True)
                        last.then_inc(y_cb, 1)
                    elif step == "xs_t":
                        pe.wait_ge(y_xs, 4)
                        pe.wait_ge(y_cb_read, 1)
                        for q in range(4):
                            b, half = q // 2, q % 2
                            for t in range(4):
                                last = pe.transpose(PS[q][:, t * P:(t + 1) * P], XS[:, 4 * half + t, b * P:(b + 1) * P],
                                                    ident[:, :])
                            last.then_inc(y_xst, 1)
                    elif step == "dt":
                        if k == 0:
                            for b in range(TB):
                                for kt in range(KT):
                                    for x, h in enumerate((h_hi, h_lo)):
                                        last = pe.matmul(MISC[:, 16 * b:16 * b + 16], h[:, kt, b * P:(b + 1) * P].bitcast(F32),
                                                         w_dt[:, kt, :], start=(kt + x == 0), stop=(kt + x == KT))
                            last.then_inc(y_dt, 1)
                        elif k == 2:
                            pe.wait_ge(y_dta, 1)
                            two_blocks(MISC[0:SSD_H, :], dta[:, 0, :], dta[:, 1, :], causal).then_inc(y_dt_r, 1)
                        elif k == 3:
                            pe.wait_ge(y_acs, 1)
                            for b in range(TB):
                                last = pe.transpose(MISC[:, 288 + 16 * b:304 + 16 * b], acs_r[:, b * P:(b + 1) * P],
                                                    ident[0:SSD_H, 0:SSD_H])
                            last.then_inc(y_dt_r, 1)
                    elif step == "decay":
                        if k == 0:
                            pe.wait_ge(proj_ready, st["evac"] + 18)
                            pe.wait_ge(y_acs, 2)
                        if k >= 2:
                            pe.wait_ge(y_e, k - 1)
                        for x in range(2):
                            h = 2 * k + x
                            last = pe.matmul(PS[4 + k % 2][:, x * T:x * T + T],
                                             ident[0:SSD_H, h:h + 1].broadcast_to([SSD_H, P]), acs_r,
                                             start=True, stop=True)
                        last.then_inc(y_r, 1)
                    elif step == "head":
                        pe.wait_ge(y_w, k + 1)
                        if k == 0:
                            pe.wait_ge(y_xc, 4)
                        if k >= 2:
                            pe.wait_ge(y_y, k - 1)
                        e = decay_of(k)
                        c = slice(k * P, (k + 1) * P)
                        for x in range(2):
                            last = two_blocks(PS[6 + k % 2][:, x * T:x * T + T], XC_T[:, 0, c], XC_T[:, 1, c], e[:, x, :])
                        last.then_inc(y_o, 1)
                    elif step == "norm":
                        pe.wait_ge(y_y, 8)
                        for g in range(2):
                            pe.wait_ge(y_sq, g + 1)
                            for t in range(4):
                                last = pe.matmul(MISC[:, g * T:g * T + T], ones[:, :], work[:, 4 * g + t, :],
                                                 start=(t == 0), stop=(t == 3))
                        last.then_inc(y_sum, 1)
                finish_update(st)

            def mlstm(st):
                n0, done = st["piece"], 0
                sum_squares(st["sq"])
                for step, k in mlstm_sequence():
                    if step in ("xm", "z"):
                        i = k if step == "xm" else 8 + k
                        if i >= RING:
                            pe.wait_ge(proj_ready, st["evac"] + i - 2)
                        project(n0 + i, norm=st["norm"] if i == 0 else None)
                    if step == "xm":
                        for t in (2 * k, 2 * k + 1):
                            pe.wait_ge(m_bd, t + 1)
                            g = slice(t % 8 * 36, t % 8 * 36 + 36)
                            pe.matmul(PS[t // 8][:, g], BD[:, t % 2, 0, :], WG[:, t, :], start=True, stop=False)
                            pe.matmul(PS[t // 8][:, g], BD[:, t % 2, 1, :], WG[:, 16 + t, :], start=False, stop=True)
                            pe.matmul(PS[2 + t // 8][:, g], BD[:, t % 2, 2, :], WG[:, 32 + t, :], start=True,
                                      stop=True).then_inc(m_bd_used, 1)
                    elif step == "gates":
                        pe.wait_ge(m_gsb, 1)
                        pe.wait_ge(m_xc, 8)
                        for t in range(16):
                            pe.matmul(MISC[0:36, 0:T], GE[:, t, :], XC[:, t, :], start=(t == 0), stop=False)
                            last = pe.matmul(MISC[0:36, 0:T], GE[:, 16 + t, :], xm_in[:, t, :], start=False, stop=(t == 15))
                        last.then_inc(m_gates, 1)
                    elif step == "cols":
                        pe.wait_ge(m_rowd, 2)
                        for b in range(TB):
                            last = pe.transpose(PS[2][:, MH * b:MH * b + MH], i_row[:, b * P:(b + 1) * P],
                                                ident[0:MH, 0:MH])
                        last.then_inc(m_colT, 1)
                    elif step == "a":
                        if k:
                            pe.wait_ge(m_w, k)
                            pe.wait_ge(m_absd, k)
                        else:
                            pe.wait_ge(m_rows, 4)
                        for t in range(4):
                            n, tile = 4 * k + t, 4 * k + t
                            pe.wait_ge(m_bd, 16 + n + 1)
                            if t:
                                pe.wait_ge(m_qks, n)
                            pe.matmul(PS[0][:, 0:T], BD[:, n % 2, 0, :], XC[:, tile, :], start=True, stop=True)
                            pe.matmul(PS[0][:, T:2 * T], BD[:, n % 2, 1, :], XC[:, tile, :], start=True,
                                      stop=True).then_inc(m_qk, 1)
                            if t == 2:
                                pe.wait_ge(m_vs, 2 * k + 1)
                            for b in range(TB):
                                c = (t % 2) * T + b * P
                                last = pe.matmul(PS[2][:, c:c + P], xm_in[:, tile, b * P:(b + 1) * P],
                                                 BD[:, n % 2, 2, :], start=True, stop=True)
                            last.then_inc(m_bd_used, 1)
                    elif step == "b":
                        pe.wait_ge(m_rows, 3)
                        if k:
                            pe.wait_ge(m_absd, k)
                        pick = ident[0:MH, k:k + 1].broadcast_to([MH, P])
                        pe.matmul(PS[1][:, 0:T], pick, m_row, start=True, stop=True)
                        pe.matmul(PS[1][:, T:2 * T], pick, em_row, start=True, stop=True).then_inc(m_mb, 1)
                        pe.wait_ge(m_qks, 4 * k + 4)
                        for d in range(4):
                            pe.matmul(PS[0][:, 0:T], QK[:, d, T:T + P], QK[:, d, 0:T], start=(d == 0), stop=(d == 3))
                        for d in range(4):
                            last = pe.matmul(PS[0][:, T:384], QK[:, d, T + P:2 * T], QK[:, d, P:T], start=(d == 0),
                                             stop=(d == 3))
                        last.then_inc(m_s, 1)
                    elif step == "c":
                        pe.wait_ge(m_w, k + 1)
                        pe.wait_ge(m_vs, 2 * k + 2)
                        two_blocks(PS[2], ones[:, :], ones[:, :], WW).then_inc(m_den, 1)
                        if k:
                            pe.wait_ge(m_hh, k)
                        for t in range(4):
                            bank = (PS[3], MISC)[t // 2][:, (t % 2) * T:(t % 2 + 1) * T]
                            c = slice(t * P, (t + 1) * P)
                            last = two_blocks(bank, VH[:, 0, c], VH[:, 1, c], WW)
                        last.then_inc(m_num, 1)
                    elif step == "d":
                        pe.wait_ge(m_hh, k + 1)
                        if k + 1 < MH:
                            pe.wait_ge(m_vs, 2 * (k + 1) + 2)
                        for t in range(4):
                            last = pe.matmul(PS[2][:, 0:T], ones[:, :], xm_in[:, 4 * k + t, :], start=(t == 0),
                                             stop=(t == 3))
                        last.then_inc(m_mean, 1)
                    elif step == "e":
                        pe.wait_ge(m_hc, 2 * k + 2)
                        for t, buf in enumerate((gate_f, gate_f, hid_f, hid_f)):
                            if t % 2 == 0:
                                pe.wait_ge(m_sq, 2 * k + t // 2 + 1)
                            last = pe.matmul(PS[2][:, 0:T], ones[:, :], buf[:, (t % 2) * T:(t % 2 + 1) * T],
                                             start=(t == 0), stop=(t == 3))
                        last.then_inc(m_var, 1)
                pe.wait_ge(m_rs, MH)
                down_all(st)
                finish_update(st)

            def ffn(st):
                n, c0 = st["piece"], CHUNKS * st["ffn"]
                sum_squares(st["sq"])
                project(n, norm=st["norm"])
                project(n + 1)

                def body(n0, i, c, first):
                    pe.wait_ge(silu_ready, c)
                    project(n0, i)
                    pe.wait_ge(hid_full, c)
                    project(n0 + 1, i)
                    pe.wait_ge(hid_ready, c)
                    down(n0 + 2, i, 0, first, False)

                body(n + 2, None, c0 + 1, True)
                with pe.Fori(1, CHUNKS - 1) as i:
                    body(n + 2, i, i + (c0 + 1), False)
                next_columns(st)
                pe.wait_ge(hid_ready, c0 + CHUNKS)
                down(n + 3 * CHUNKS - 1, None, 0, False, True)
                finish_update(st)

            pe.wait_ge(const_ready, 3)
            pe.wait_ge(in_loaded, 16)
            for r in range(ROW_TILES):
                if r >= 4:
                    pe.wait_ge(cols_ready, r - 3)
                pe.transpose(PS[r % 4][:, 0:P], rows_in[:, r, :], ident[:, :]).then_inc(rowsT, 1)
            pe.wait_ge(cols_ready, ROW_TILES)

            def turn_x():
                pe.wait_ge(x_loaded, 16)
                for kt in range(KT):
                    for b in range(TB):
                        c = (kt % 2) * T + b * P
                        last = pe.transpose(PS[4 + kt // 2][:, c:c + P], x_in[:, b, kt * P:(kt + 1) * P], ident[:, :])
                    if kt % 2:
                        last.then_inc(xin_T, 1)

            if not plan.subs:
                turn_x()
            else:
                pe.wait_ge(c_ready, 1)
                for n in range(8):
                    if n == 3:
                        turn_x()
                    pe.wait_ge(first_loaded[n % FIRST_SLOTS], 16 * (n // FIRST_SLOTS + 1))
                    w = first_w[:, n % FIRST_SLOTS, :].rearrange("p (k n) -> p k n", k=KT)
                    for kt in range(KT):
                        last = pe.matmul(PS[n // 2][0:1, n % 2 * 256:n % 2 * 256 + 256], c_act[:, kt:kt + 1], w[:, kt, :],
                                         start=(kt == 0), stop=(kt == KT - 1))
                    last.then_inc(first_used, 1)
                pe.wait_ge(first_copied, 4)
                for j in range(16):
                    last = pe.matmul(PS[0][:, j:j + 1], first_row[:, j * P:(j + 1) * P], ones[0:1, 0:1],
                                     start=True, stop=True)
                last.then_inc(first_cols, 1)
            pe.wait_ge(masks_ready, 1)
            pe.wait_ge(xt_ready, KT)
            done_subs = 0
            for st in plan.steps:
                kind, idx = st["key"]
                if st["key"] in SUB:
                    done_subs += 1
                    if done_subs > 1:
                        pe.wait_ge(mod_ready, done_subs)
                if kind == "ffn":
                    ffn(st)
                elif kind in "ABC":
                    attention(st)
                elif kind == "mlstm":
                    mlstm(st)
                elif kind == "hyb":
                    hybrid(st)
                if st["key"] == ("ffn", 3):
                    sum_squares(st["sq"] + 1)
            for b in range(TB):
                for kt in range(KT):
                    if b == 0:
                        pe.wait_ge(xt_ready, 8 * plan.updates + kt + 1)
                    q = 2 * b + kt // 4
                    last = pe.transpose(PS[4 + q][:, (kt % 4) * P:(kt % 4 + 1) * P], XT[:, kt, b * P:(b + 1) * P],
                                        ident[:, :])
                    if kt % 4 == 3:
                        last.then_inc(outT, 1)


def columns_first(w):
    k, n = w.shape
    return w.reshape(k // P, P, n // 256, 256).transpose(2, 1, 0, 3).reshape(n // 256, P, PIECE)


def rows_first(w):
    r = w.shape[0]
    return w.reshape(r // 256, 2, P, D).transpose(0, 2, 1, 3).reshape(r // 256, P, PIECE)


def ffn_pieces(g, u, d):
    g, u, d = columns_first(g), columns_first(u), rows_first(d)
    order = [g[0], u[0]]
    for c in range(1, CHUNKS):
        order += [g[c], u[c], d[c - 1]]
    return order + [d[CHUNKS - 1]]


def stream(x, stages):
    order = []
    for kind, k in stages:
        if kind == "ffn":
            if k < 4:
                g, u, d = (x[n][k // 2, k % 2] for n in ("ffn_w_gate", "ffn_w_up", "ffn_w_down"))
            else:
                g, u, d = (x[n][k - 4] for n in ("ffn_w_gate_2", "ffn_w_up_2", "ffn_w_down_2"))
            order += ffn_pieces(g, u, d)
        elif kind in "AB":
            w = columns_first(x[f"{kind.lower()}_w_in_2"][k])
            order += [w[8], w[9], w[10], w[11]]
            for j in range(4):
                order += [w[j], w[4 + j]]
            order += list(rows_first(x[f"{kind.lower()}_w_out_2"][k]))
        elif kind == "hyb":
            w = x["hyb_w_in"][0]
            for first, last in ((D, 2 * D), (0, D), (4 * D, 4 * D + 512), (3 * D, 4 * D), (2 * D, 3 * D)):
                order += list(columns_first(w[:, first:last]))
            order += list(rows_first(x["hyb_w_out"][0]))
        elif kind == "mlstm":
            order += list(columns_first(x["mlstm_w_up"][0])) + list(rows_first(x["mlstm_w_down"][0]))
        elif kind == "C":
            w = columns_first(x["c_w_in_2"][k])
            order += [w[4], w[0], w[1], w[2], w[3]] + list(rows_first(x["c_w_out_2"][k]))
    return np.stack(order)


def arrays(x, stages):
    rows = np.concatenate([x[n].reshape(-1, P) for n, _ in ROWS])
    w4 = [x[n][0] for n in ("mlstm_wq", "mlstm_wk", "mlstm_wv")]
    w4 = np.stack([w.reshape(16, P, 4) for w in w4 + [w.transpose(0, 2, 1) for w in w4]]).transpose(2, 0, 1, 3)
    wg = np.zeros((P, 48, 36), np.float32)
    gates = x["mlstm_w_gates"][0].reshape(48, P, 2 * MH).transpose(1, 0, 2)
    wg[:, :, 0:MH], wg[:, :, 32:36] = gates[:, :, 0:MH], gates[:, :, MH:]
    rows = np.concatenate([rows, np.zeros((ROW_TILES * P - rows.shape[0], P), np.float32)])
    w_dt = x["hyb_w_in"][0][:, 4 * D + 512:].reshape(KT, P, SSD_H).transpose(1, 0, 2).reshape(P, KT * SSD_H)
    small_h = [w_dt, np.repeat(x["ssd_d"][0].reshape(KT, 2), 64, axis=1).transpose(1, 0),
               np.tile(x["ssd_dt_bias"], (P, 1)), np.tile(x["ssd_a_log"], (P, 1))]
    out = {
        "small_h": np.concatenate(small_h, axis=1),
        "wax": np.stack([x["lru_wa"][0], x["lru_wx"][0]]).transpose(2, 0, 1, 3).reshape(P, 2 * 8 * P),
        "x": x["x"].reshape(T, D),
        "rows": np.ascontiguousarray(rows.reshape(ROW_TILES, P, P).transpose(1, 0, 2)),
        "ada": np.concatenate([columns_first(w) for w in x["ada_w"]]),
        "ws": stream(x, stages),
        "inv_freq": np.tile(np.float32(10000.0) ** (-np.arange(0, 64, 2, dtype=np.float32) / np.float32(64)),
                            4).reshape(P, 1).astype(np.float32),
        "w4": w4.reshape(P, 6 * 16 * 4),
        "wg": wg.reshape(P, 48 * 36),
        "b_gate": x["mlstm_b_gates"].reshape(2, MH).transpose(1, 0),
        "positions": x["positions_2"].reshape(T),
        "sinks": x["c_sinks_2"].reshape(16),
        "lambda": x["a_lambda_2"].reshape(2 * 4 * 64),
    }
    return {k: np.ascontiguousarray(v) for k, v in out.items()}


def kernel(**inputs):
    from concourse import bacc
    from concourse.bass_utils import run_bass_kernel_spmd

    nc = bacc.Bacc("TRN2", target_bir_lowering=False, num_devices=1, dynamic_dma_scratch_size=2048)
    data = {f"in_{k}": v for k, v in arrays({k: np.asarray(v) for k, v in inputs.items()}, STAGES).items()}
    aps = {k[3:]: nc.dram_tensor(k, v.shape, mybir.dt.from_np(v.dtype), kind="ExternalInput").ap()
           for k, v in data.items()}
    out = nc.dram_tensor("out_y", (T, D), F32, kind="ExternalOutput").ap()
    build(nc, aps, out, STAGES)
    result = run_bass_kernel_spmd(nc, [data], core_ids=[0])
    return result.results[0]["out_y"].reshape(1, T, D)
```
